# Optimizing a Trainium2 kernel written in Bass

```python
import math
import jax
import jax.numpy as jnp
from jax import lax
import numpy as np

D_MODEL = 1024
BATCH = 1
SEQ = 128
DEPTH = 1
DEC_BATCH = 1
DEC_SEQ = 2048
PAST_LEN = 128

GRID_W = 64
D_MIX = D_MODEL
D_RNN = D_MIX // 2
D_HY = D_MIX - D_RNN
N_RNN_HEADS = 8
RNN_HEAD_DIM = D_RNN // N_RNN_HEADS
RG_CONV_W = 4
RG_C = 8.0
HY_CONV_W = 3
HY_ORDER = 2
HY_BANDS = 16
HY_EMB = 1 + 2 * HY_BANDS
HY_FH = 64
HY_DECAY_TARGET = 1e-2
HY_DECAY_PCT_SHORT = 0.3
HY_DECAY_PCT_LONG = 1.5
D_FF = ((8 * D_MODEL // 3 + 127) // 128) * 128
FFN_CONV_W = 3
D_IN = 2 * D_RNN + 3 * D_HY
N_MOD = 6
EPS = 1e-6

kernel_name = 'hymba_rglru_hyena_prefix_dit_step'

def rms_norm(x, g):
    x32 = x.astype(jnp.float32)
    y = x32 * lax.rsqrt(jnp.mean(x32 * x32, axis=-1, keepdims=True) + EPS)
    return y.astype(x.dtype) * g

def dwconv1d(x, w, b):
    K = w.shape[0]
    L = x.shape[1]
    left = K // 2
    xp = jnp.pad(x, ((0, 0), (left, K - 1 - left), (0, 0)))
    out = xp[:, 0:L] * w[0]
    for k in range(1, K):
        out = out + xp[:, k:k + L] * w[k]
    return out + b

def dwconv2d_grid(x, w, b):
    B, L, C = x.shape
    rows = L // GRID_W
    xg = x.reshape(B, rows, GRID_W, C)
    y = lax.conv_general_dilated(xg, w[:, :, None, :], window_strides=(1, 1), padding='SAME',
                                 dimension_numbers=('NHWC', 'HWIO', 'NHWC'), feature_group_count=C)
    return y.reshape(B, L, C) + b

def _lin_combine(e1, e2):
    a1, b1 = e1
    a2, b2 = e2
    return a1 * a2, a2 * b1 + b2

def rglru(x, h0, gate_w, gate_b, a_param, reverse):
    B, L, _ = x.shape
    x32 = x.astype(jnp.float32)
    xh = x32.reshape(B, L, N_RNN_HEADS, RNN_HEAD_DIM)
    g = jnp.einsum('blhi,ghij->gblhj', xh, gate_w.astype(jnp.float32)).reshape(2, B, L, D_RNN)
    g = g + gate_b.astype(jnp.float32)[:, None, None, :]
    r = jax.nn.sigmoid(g[0])
    i = jax.nn.sigmoid(g[1])
    log_a = -RG_C * r * jax.nn.softplus(-a_param.astype(jnp.float32))
    a = jnp.exp(log_a)
    b = x32 * i * jnp.sqrt(-jnp.expm1(2.0 * log_a))
    A, Bc = lax.associative_scan(_lin_combine, (a, b), reverse=reverse, axis=1)
    return A * h0.astype(jnp.float32)[:, None, :] + Bc

def hyena_filter_fft(L, w1, b1, w2, b2, w3, freq):
    f32 = jnp.float32
    pos = jnp.arange(L, dtype=f32)
    t = pos / max(L - 1, 1)
    omega = 2.0 * math.pi * pos / L
    bands = jnp.linspace(1e-4, HY_BANDS - 1, HY_BANDS, dtype=f32)
    ang = omega[:, None] * bands[None, :]
    feats = jnp.concatenate([t[:, None], jnp.cos(ang), jnp.sin(ang)], axis=-1)
    fr = freq.astype(f32)
    h = jnp.sin(fr[0] * (feats @ w1.astype(f32) + b1.astype(f32)))
    h = jnp.sin(fr[1] * (h @ w2.astype(f32) + b2.astype(f32)))
    h = (h @ w3.astype(f32)).reshape(L, HY_ORDER, 2, D_HY)
    min_decay = math.log(HY_DECAY_TARGET) / HY_DECAY_PCT_LONG
    max_decay = math.log(HY_DECAY_TARGET) / HY_DECAY_PCT_SHORT
    deltas = jnp.abs(jnp.linspace(min_decay, max_decay, D_HY, dtype=f32))
    h = h * jnp.exp(-t[:, None] * deltas[None, :])[:, None, None, :]
    h_fwd = h[:, :, 0]
    h_bwd = h[:, :, 1]
    circ = jnp.concatenate([h_fwd, jnp.zeros((1, HY_ORDER, D_HY), f32), h_bwd[:0:-1]], axis=0)
    return jnp.fft.rfft(circ, axis=0)

def fft_long_conv(u, k_f, bias):
    L = u.shape[1]
    U = jnp.fft.rfft(u, n=2 * L, axis=1)
    y = jnp.fft.irfft(U * k_f[None], n=2 * L, axis=1)[:, :L]
    return y + u * bias.astype(jnp.float32)

def trunk_layer(x, mod, h0_f, h0_b, p, on_grid):
    shift1, scale1, gate1, shift2, scale2, gate2 = jnp.split(mod[:, None, :], N_MOD, axis=-1)
    xn = rms_norm(x, p['g_norm1']) * (1 + scale1) + shift1
    proj = xn @ p['w_in']
    x_r = proj[..., :D_RNN]
    y_r = proj[..., D_RNN:2 * D_RNN]
    hy_in = proj[..., 2 * D_RNN:]
    xc = dwconv1d(x_r, p['rg_conv_w'], p['rg_conv_b'])
    h_f = rglru(xc, h0_f, p['rg_gate_w'][0], p['rg_gate_b'][0], p['rg_a'][0], False)
    h_b = rglru(xc, h0_b, p['rg_gate_w'][1], p['rg_gate_b'][1], p['rg_a'][1], True)
    o_r = ((h_f + h_b) * jax.nn.gelu(y_r.astype(jnp.float32))).astype(x.dtype)
    hy = dwconv1d(hy_in, p['hy_conv_w'], p['hy_conv_b']).astype(jnp.float32)
    v, x1, x2 = jnp.split(hy, 3, axis=-1)
    k_f = hyena_filter_fft(x.shape[1], p['hf_w1'], p['hf_b1'], p['hf_w2'], p['hf_b2'], p['hf_w3'], p['hf_freq'])
    z = x1 * fft_long_conv(v, k_f[:, 0], p['hy_bias'][0])
    z = x2 * fft_long_conv(z, k_f[:, 1], p['hy_bias'][1])
    o_h = z.astype(x.dtype)
    o = jnp.concatenate([rms_norm(o_r, p['g_rnn_out']), rms_norm(o_h, p['g_hy_out'])], axis=-1) @ p['w_out']
    x = x + gate1 * o
    xn2 = rms_norm(x, p['g_norm2']) * (1 + scale2) + shift2
    a_ff, g_ff = jnp.split(xn2 @ p['w_up'], 2, axis=-1)
    if on_grid:
        g_ff = dwconv2d_grid(g_ff, p['ffn_conv_w'], p['ffn_conv_b'])
    else:
        g_ff = dwconv1d(g_ff, p['ffn_conv_w'][1], p['ffn_conv_b'])
    x = x + gate2 * ((jax.nn.gelu(g_ff) * a_ff) @ p['w_down'])
    return x, h_f[:, -1], h_b[:, 0]

def setup_inputs(seed: int = 0) -> dict:
    key = jax.random.key(seed)
    ks = iter(jax.random.split(key, 48))

    def nrm(shape, scale):
        return scale * jax.random.normal(next(ks), shape, jnp.float32)

    x_prompt = nrm((BATCH, SEQ, D_MODEL), 1.0)
    x_sample = nrm((DEC_BATCH, DEC_SEQ, D_MODEL), 1.0)
    state_rglru = nrm((DEC_BATCH, DEPTH, 2, D_RNN), 0.5)
    c = nrm((DEC_BATCH, D_MODEL), 1.0)
    c_ctx = nrm((D_MODEL,), 1.0)
    w_ada = nrm((DEPTH, D_MODEL, N_MOD * D_MODEL), 0.5 * D_MODEL ** -0.5)
    b_ada = nrm((DEPTH, N_MOD * D_MODEL), 0.02)
    g_norm1 = 1.0 + nrm((DEPTH, D_MODEL), 0.02)
    g_norm2 = 1.0 + nrm((DEPTH, D_MODEL), 0.02)
    w_in = nrm((DEPTH, D_MODEL, D_IN), D_MODEL ** -0.5)
    rg_conv_w = nrm((DEPTH, RG_CONV_W, D_RNN), RG_CONV_W ** -0.5)
    rg_conv_b = nrm((DEPTH, D_RNN), 0.02)
    rg_gate_w = nrm((DEPTH, 2, 2, N_RNN_HEADS, RNN_HEAD_DIM, RNN_HEAD_DIM), RNN_HEAD_DIM ** -0.5)
    rg_gate_b = nrm((DEPTH, 2, 2, D_RNN), 0.02)
    u = jax.random.uniform(next(ks), (DEPTH, 2, D_RNN), jnp.float32, 0.9, 0.999)
    a_base = u ** (1.0 / RG_C)
    rg_a = jnp.log(a_base) - jnp.log1p(-a_base)
    hy_conv_w = nrm((DEPTH, HY_CONV_W, 3 * D_HY), HY_CONV_W ** -0.5)
    hy_conv_b = nrm((DEPTH, 3 * D_HY), 0.02)
    hf_w1 = nrm((DEPTH, HY_EMB, HY_FH), HY_EMB ** -0.5)
    hf_b1 = nrm((DEPTH, HY_FH), 0.1)
    hf_w2 = nrm((DEPTH, HY_FH, HY_FH), HY_FH ** -0.5)
    hf_b2 = nrm((DEPTH, HY_FH), 0.1)
    hf_w3 = nrm((DEPTH, HY_FH, HY_ORDER * 2 * D_HY), HY_FH ** -0.5)
    hf_freq = 1.0 + nrm((DEPTH, 2, HY_FH), 0.1)
    hy_bias = nrm((DEPTH, HY_ORDER, D_HY), 0.5)
    g_rnn_out = 1.0 + nrm((DEPTH, D_RNN), 0.02)
    g_hy_out = 1.0 + nrm((DEPTH, D_HY), 0.02)
    w_out = nrm((DEPTH, D_MIX, D_MODEL), D_MIX ** -0.5)
    w_up = nrm((DEPTH, D_MODEL, 2 * D_FF), D_MODEL ** -0.5)
    ffn_conv_w = nrm((DEPTH, FFN_CONV_W, FFN_CONV_W, D_FF), 1.0 / FFN_CONV_W)
    ffn_conv_b = nrm((DEPTH, D_FF), 0.02)
    w_down = nrm((DEPTH, D_FF, D_MODEL), D_FF ** -0.5)
    g_final = 1.0 + nrm((D_MODEL,), 0.02)
    return {'x_prompt': x_prompt, 'x_sample': x_sample, 'state_rglru': state_rglru, 'c': c, 'c_ctx': c_ctx,
            'w_ada': w_ada, 'b_ada': b_ada, 'g_norm1': g_norm1, 'g_norm2': g_norm2, 'w_in': w_in,
            'rg_conv_w': rg_conv_w, 'rg_conv_b': rg_conv_b, 'rg_gate_w': rg_gate_w, 'rg_gate_b': rg_gate_b,
            'rg_a': rg_a, 'hy_conv_w': hy_conv_w, 'hy_conv_b': hy_conv_b, 'hf_w1': hf_w1, 'hf_b1': hf_b1,
            'hf_w2': hf_w2, 'hf_b2': hf_b2, 'hf_w3': hf_w3, 'hf_freq': hf_freq, 'hy_bias': hy_bias,
            'g_rnn_out': g_rnn_out, 'g_hy_out': g_hy_out, 'w_out': w_out, 'w_up': w_up,
            'ffn_conv_w': ffn_conv_w, 'ffn_conv_b': ffn_conv_b, 'w_down': w_down, 'g_final': g_final}

def reference(x_prompt, x_sample, state_rglru, c, c_ctx, w_ada, b_ada, g_norm1, g_norm2, w_in,
              rg_conv_w, rg_conv_b, rg_gate_w, rg_gate_b, rg_a, hy_conv_w, hy_conv_b, hf_w1, hf_b1,
              hf_w2, hf_b2, hf_w3, hf_freq, hy_bias, g_rnn_out, g_hy_out, w_out, w_up,
              ffn_conv_w, ffn_conv_b, w_down, g_final):
    xp = x_prompt
    xs = x_sample
    zero_h = jnp.zeros((x_prompt.shape[0], D_RNN), jnp.float32)
    new_states = []
    for l in range(DEPTH):
        p = {'g_norm1': g_norm1[l], 'g_norm2': g_norm2[l], 'w_in': w_in[l],
             'rg_conv_w': rg_conv_w[l], 'rg_conv_b': rg_conv_b[l], 'rg_gate_w': rg_gate_w[l],
             'rg_gate_b': rg_gate_b[l], 'rg_a': rg_a[l], 'hy_conv_w': hy_conv_w[l], 'hy_conv_b': hy_conv_b[l],
             'hf_w1': hf_w1[l], 'hf_b1': hf_b1[l], 'hf_w2': hf_w2[l], 'hf_b2': hf_b2[l], 'hf_w3': hf_w3[l],
             'hf_freq': hf_freq[l], 'hy_bias': hy_bias[l], 'g_rnn_out': g_rnn_out[l], 'g_hy_out': g_hy_out[l],
             'w_out': w_out[l], 'w_up': w_up[l], 'ffn_conv_w': ffn_conv_w[l], 'ffn_conv_b': ffn_conv_b[l],
             'w_down': w_down[l]}
        mod_ctx = jax.nn.silu(c_ctx)[None, :] @ w_ada[l] + b_ada[l]
        mod_lat = jax.nn.silu(c) @ w_ada[l] + b_ada[l]
        xp, hf_last, hb_first = trunk_layer(xp, mod_ctx, zero_h, zero_h, p, False)
        new_states.append(jnp.stack([hf_last, hb_first], axis=1).astype(x_prompt.dtype))
        xs, _, _ = trunk_layer(xs, mod_lat, state_rglru[:, l, 0], state_rglru[:, l, 1], p, True)
    y_prompt = rms_norm(xp, g_final)
    y_sample = rms_norm(xs, g_final)
    new_state_rglru = jnp.stack(new_states, axis=1)
    return (y_prompt, y_sample, new_state_rglru)


_drawn_inputs = setup_inputs


def setup_inputs(seed=0):
    import zlib

    import numpy as np

    out = dict(_drawn_inputs(seed))
    spreads = {}
    factors = {'state_rglru': 6.789,
     'g_norm1': 5.988,
     'g_norm2': 8.0,
     'rg_gate_b': 16.941,
     'g_rnn_out': 27.318,
     'g_hy_out': 24.629,
     'ffn_conv_b': 8.0,
     'g_final': 8.033,
     'rg_conv_b': 2.984}
    for name, (base, spread) in spreads.items():
        noise = np.random.default_rng([zlib.crc32(name.encode()), seed]).standard_normal(out[name].shape)
        drawn = base * np.exp(spread * noise) if base else spread * noise
        out[name] = jnp.asarray(drawn.astype(out[name].dtype))
    for name, factor in factors.items():
        out[name] = (out[name] * factor).astype(out[name].dtype)
    return out
```

```python
import math
from contextlib import ExitStack

import numpy as np

import concourse.bass as bass
from concourse import mybir
from concourse.alu_op_type import AluOpType as ALU

F32 = mybir.dt.float32
F32R = mybir.dt.float32r
ACT = mybir.ActivationFunctionType

P = 128
D_MODEL = 1024
KM = D_MODEL // P
SEQ_LAT, SEQ_CTX = 2048, 128
T = SEQ_LAT + SEQ_CTX
GRID_W = 64
GRID_H = SEQ_LAT // GRID_W
D_RNN = D_HY = 512
CT = D_RNN // P
D_FF = 2816
KF = D_FF // P
HY_BANDS = 16
N_MOD = 6
EPS = 1e-6
RG_C = 8.0
N_CONV = 4 * CT
N_IN = 5 * CT
TOKEN_BLOCKS = [(0, 448), (448, 448), (896, 448), (1344, 448), (1792, 384)]
NB = len(TOKEN_BLOCKS)
CTX_AT = SEQ_LAT
POS_LAT, POS_CTX = 2 * SEQ_LAT, 2 * SEQ_CTX
POS = POS_LAT + POS_CTX
POS_BLOCKS = [(s, min(512, POS - s)) for s in range(0, POS, 512)]
ROW_TILES = POS // P
PARAMS = {}
for _name, _width in (("g1", KM), ("g2", KM), ("go", KM), ("gf", KM), ("cw", 4 * N_CONV), ("cb", N_CONV),
                      ("gate_b", 4 * CT), ("rg_a", 2 * CT), ("h0", 2 * CT), ("hy_b", 2 * CT),
                      ("ffn_w", 9 * KF), ("ffn_b", KF), ("mlp_b", 2), ("mlp_f", 2)):
    PARAMS[_name] = (sum(w for _, w in PARAMS.values()), _width)
N_PARAMS = sum(w for _, w in PARAMS.values())
SHIFT1, SCALE1, GATE1, SHIFT2, SCALE2, GATE2 = (KM * j for j in range(N_MOD))
LAT, CTX = 0, 1
PAD_AT_LAT, PAD_AT_CTX = 2, 2 + SEQ_LAT + 3
PAD_LEN = PAD_AT_CTX + SEQ_CTX + 1


class Steps:

    def __init__(self, engine, sem, start=0):
        self.engine, self.sem, self.start, self.n = engine, sem, start, 0

    def done(self, instruction):
        self.n += 1
        instruction.then_inc(self.sem, 1)

    def wait(self):
        self.engine.wait_ge(self.sem, self.start + self.n)


def segments(start, width):
    cut = min(max(CTX_AT, start), start + width)
    return [(s, w, m) for s, w, m in ((start, cut - start, LAT), (cut, start + width - cut, CTX)) if w]



def norm_semaphores(sem):
    names = ["squared", "summed", "mean_ready", "inverse_ready", "rstd_ready", "scaled_ready", "hi_ready", "lo_ready"]
    sems = {name: sem("norm_" + name) for name in names}
    sems.update({f"x_loaded{k}": sem(f"norm_x_loaded{k}") for k in range(KM)})
    return sems, {name: 0 for name in sems}


def norm_buffers(sb, psum, norm_sems, tag, groups):
    sems, starts = norm_sems
    at_start = dict(starts)
    for name in starts:
        starts[name] += NB * (16 if name.startswith("x_loaded") else groups if name in
                              ("mean_ready", "inverse_ready", "rstd_ready") else KM)
    return {
        "groups": groups,
        "x": sb(tag + "_norm_x", [P, KM, 448], F32),
        "square": sb(tag + "_norm_square", [P, 2, 448], F32),
        "rstd": sb(tag + "_norm_rstd", [P, groups, 448], F32),
        "scaled": sb(tag + "_norm_scaled", [P, 2, 448], F32),
        "psum": psum(tag + "_norm_psum", [P, groups, 512], F32),
        "sems": sems,
        "start": at_start,
    }


def norm_wait(engine, nb, name, count):
    engine.wait_ge(nb["sems"][name], nb["start"][name] + count)


def norm_loads(sp, nb, source):
    for b, (s, w) in enumerate(TOKEN_BLOCKS):
        for k in range(KM):
            if b:
                norm_wait(sp, nb, "scaled_ready", KM * (b - 1) + k + 1)
            sp.dma_start(nb["x"][:, k, :w], source[k][:, s:s + w]).then_inc(nb["sems"][f"x_loaded{k}"], 16)


def norm_scalar(nc, act, nb, shift, xh):
    for b, (s, w) in enumerate(TOKEN_BLOCKS):
        for k in range(KM):
            n = KM * b + k
            norm_wait(act, nb, f"x_loaded{k}", 16 * (b + 1))
            if n >= 2:
                norm_wait(act, nb, "summed", n - 1)
            nc.scalar.activation(nb["square"][:, n % 2, :w], nb["x"][:, k, :w], ACT.Square)\
              .then_inc(nb["sems"]["squared"], 1)
        for g in range(nb["groups"]):
            norm_wait(act, nb, "inverse_ready", nb["groups"] * b + g + 1)
            nc.scalar.activation(nb["rstd"][:, g, :w], nb["rstd"][:, g, :w], ACT.Sqrt)\
              .then_inc(nb["sems"]["rstd_ready"], 1)
        for k in range(KM):
            n = KM * b + k
            norm_wait(act, nb, "scaled_ready", n + 1)
            for at, width, m in segments(s, w):
                if shift is None:
                    hi = nc.scalar.activation(xh[:, k, at:at + width], nb["scaled"][:, n % 2, at - s:at - s + width],
                                              ACT.Copy)
                else:
                    hi = nc.scalar.activation(xh[:, k, at:at + width], nb["scaled"][:, n % 2, at - s:at - s + width],
                                              ACT.Identity, bias=shift[:, k, m:m + 1])
            hi.then_inc(nb["sems"]["hi_ready"], 1)


def norm_vector(nc, dve, nb, scale, shift, xh, xl):
    per_group = KM // nb["groups"]
    for b, (s, w) in enumerate(TOKEN_BLOCKS):
        for g in range(nb["groups"]):
            n = nb["groups"] * b + g
            norm_wait(dve, nb, "summed", KM * b + per_group * (g + 1))
            if b:
                norm_wait(dve, nb, "scaled_ready", KM * b)
            nc.vector.tensor_scalar(nb["rstd"][:, g, :w], nb["psum"][:, g, :w], 1.0 / (P * per_group), EPS,
                                    ALU.mult, ALU.add).then_inc(nb["sems"]["mean_ready"], 1)
            norm_wait(dve, nb, "mean_ready", n + 1)
            nc.vector.reciprocal(nb["rstd"][:, g, :w], nb["rstd"][:, g, :w]).then_inc(nb["sems"]["inverse_ready"], 1)
        def lo_part(k):
            n = KM * b + k
            norm_wait(dve, nb, "hi_ready", n + 1)
            for at, width, m in segments(s, w):
                scaled = nb["scaled"][:, n % 2, at - s:at - s + width]
                hi = xh[:, k, at:at + width].bitcast(F32)
                if shift is None:
                    lo = nc.vector.tensor_tensor(xl[:, k, at:at + width], scaled, hi, ALU.subtract)
                else:
                    lo = nc.vector.scalar_tensor_tensor(out=xl[:, k, at:at + width], in0=scaled,
                                                        scalar=shift[:, k, m:m + 1], in1=hi,
                                                        op0=ALU.add, op1=ALU.subtract)
            lo.then_inc(nb["sems"]["lo_ready"], 1)

        for k in range(KM):
            n = KM * b + k
            g = k // per_group
            norm_wait(dve, nb, "rstd_ready", nb["groups"] * b + g + 1)
            if n >= 2:
                norm_wait(dve, nb, "lo_ready", n - 1)
            for at, width, m in segments(s, w):
                last = nc.vector.scalar_tensor_tensor(
                    out=nb["scaled"][:, n % 2, at - s:at - s + width], in0=nb["x"][:, k, at - s:at - s + width],
                    scalar=scale[:, k, m:m + 1], in1=nb["rstd"][:, g, at - s:at - s + width],
                    op0=ALU.mult, op1=ALU.mult)
            last.then_inc(nb["sems"]["scaled_ready"], 1)
            if k:
                lo_part(k - 1)
        lo_part(KM - 1)


def norm_tensor(pe, nb, ones):
    per_group = KM // nb["groups"]
    for b, (s, w) in enumerate(TOKEN_BLOCKS):
        if b:
            norm_wait(pe, nb, "mean_ready", nb["groups"] * b)
        for k in range(KM):
            norm_wait(pe, nb, "squared", KM * b + k + 1)
            pe.matmul(nb["psum"][:, k // per_group, :w], ones[:], nb["square"][:, (KM * b + k) % 2, :w],
                      start=(k % per_group == 0), stop=(k % per_group == per_group - 1)).then_inc(nb["sems"]["summed"], 1)



def weight_buffers(sb, sem, zero, tag):
    return {
        "zero": zero[:].unsqueeze(2).broadcast_to([P, KM, P]),
        "whole": sb(tag + "_w_whole", [P, KM, P], F32),
        "hi": sb(tag + "_w_hi", [P, 2, KM, P], F32R),
        "lo": sb(tag + "_w_lo", [P, 2, KM, P], F32R),
        "loaded": sem(f"{tag}_w_loaded"),
        "hi_ready": sem(f"{tag}_w_hi_ready"),
        "ready": sem(f"{tag}_w_ready"),
        "block_done": sem(f"{tag}_block_done"),
    }


def weight_split(nc, pool, wb, n, u, first=False):
    pool.wait_ge(wb["loaded"], n * 16 + 16)
    if not first:
        pool.wait_ge(wb["block_done"], (n - 1) * NB)
    nc.gpsimd.tensor_tensor(wb["hi"][:, u], wb["whole"][:], wb["zero"], ALU.add).then_inc(wb["hi_ready"], 1)
    pool.wait_ge(wb["hi_ready"], n + 1)
    nc.gpsimd.tensor_tensor(wb["lo"][:, u], wb["whole"][:], wb["hi"][:, u].bitcast(F32),
                            ALU.subtract).then_inc(wb["ready"], 1)


def weight_splits(nc, pool, wb, units):
    for u in range(2):
        weight_split(nc, pool, wb, u, u, first=True)
    with pool.Fori(1, units // 2) as pair:
        for u in range(2):
            weight_split(nc, pool, wb, pair * 2 + u, u)


def product_block(pe, out, wb, u, xh, xl, s, w):
    parts = [(wb["hi"], xh), (wb["hi"], xl), (wb["lo"], xh)]
    for k in range(KM):
        for j, (weight, x) in enumerate(parts):
            last = pe.matmul(out, weight[:, u, k], x[:, k, s:s + w],
                             start=(k == 0 and j == 0), stop=(k == KM - 1 and j == 2))
    last.then_inc(wb["block_done"], 1)



def modulation(nc, sem, d, keep):
    chunks, width = N_MOD * D_MODEL // 512, 512
    two_pi_hi = 6.28125
    two_pi_lo = 2 * math.pi - two_pi_hi
    round_magic = 1.5 * 2.0 ** 23
    pi_below = 3.1415925
    npos = len(POS_BLOCKS)
    sine_steps = 5
    with ExitStack() as ctx:
        def sb(name, shape, dt=F32):
            return ctx.enter_context(nc.sbuf_tensor(name, shape, dt))

        cond, act_c = sb("cond", [P, KM, 2]), sb("act_c", [P, KM, 2])
        wada = sb("wada", [P, 3, KM, width])
        bias = sb("ada_bias", [2, N_MOD * D_MODEL])
        rows = sb("mod_rows", [2, N_MOD * D_MODEL])
        work = sb("softplus_work", [P, 6, 2 * CT])
        feats = sb("feats", [P, POS])
        hidden = sb("hidden", [P, POS])
        w1, w2 = sb("mlp_w1", [P, P]), sb("mlp_w2", [P, P])
        bf = sb("mlp_bf", [P, 2])
        angle, turns = sb("angle", [P, 2, 512]), sb("turns", [P, 2, 512])
        ps = ctx.enter_context(nc.psum_tensor("mod_psum", [2, 2, 512], F32))
        turned = ctx.enter_context(nc.psum_tensor("mod_turned", [P, N_MOD * KM, 2], F32))
        ps_mlp = ctx.enter_context(nc.psum_tensor("mlp_psum", [P, 4, 512], F32))
        params, mod, scale1, scale2, sp8, nsp8, ident, ones = (keep[x] for x in (
            "params", "mod", "scale1", "scale2", "sp8", "nsp8", "ident", "ones"))
        loaded = sem("mod_loaded")
        w_loaded = [sem(f"ada_loaded{u}") for u in range(3)]
        silu_done, exp_done = sem("silu_done"), sem("exp_a_done")
        chunk_done, row_done, turn_done = sem("ada_chunk_done"), sem("ada_row_done"), sem("mod_turn_done")
        ones_done, dve_step = sem("ones_done"), sem("mod_dve_step")
        mlp_zeroed, mlp_loaded, feats_loaded = sem("mlp_zeroed"), sem("mlp_loaded"), sem("feats_loaded")
        mlp_mm, angle_ready, angle_step, turns_done, sine_done, hidden_stored = (sem(x) for x in (
            "mlp_mm", "angle_ready", "angle_step", "turns_done", "sine_done", "hidden_stored"))

        mlp_order = []
        for c in range(chunks):
            mlp_order.append([(0, c)] * (c < npos) + [(1, c - 3)] * (3 <= c < npos + 3))
        flat = [x for step in mlp_order for x in step]

        with nc.Block() as block:
            @block.sync
            def _(sp):
                for dst, src in ((cond, d["cond"]), (params, d["params"]), (bias, d["ada_bias"]), (ident, d["ident"])):
                    sp.dma_start(dst[:], src).then_inc(loaded, 16)
                sp.wait_ge(mlp_zeroed, 2)
                sp.dma_start(w1[0:1 + 2 * HY_BANDS, 0:64], d["mlp_w1"]).then_inc(mlp_loaded, 16)
                sp.dma_start(w2[0:64, 0:64], d["mlp_w2"]).then_inc(mlp_loaded, 16)
                sp.dma_start(feats[:], d["feats"]).then_inc(feats_loaded, 16)
                for c in range(chunks):
                    if c >= 3:
                        sp.wait_ge(chunk_done, c - 2)
                    sp.dma_start(wada[:, c % 3], d["w_ada"][c]).then_inc(w_loaded[c % 3], 16)
                sp.wait_ge(sine_done, 2 * npos)
                sp.dma_start(d["hidden"], hidden[:]).then_inc(hidden_stored, 16)
                sp.wait_ge(hidden_stored, 16)

            @block.scalar
            def _(act):
                act.wait_ge(loaded, 64)
                nc.scalar.activation(act_c[:], cond[:], ACT.Silu).then_inc(silu_done, 1)
                act.wait_ge(dve_step, 1)
                nc.scalar.activation(work[:, 1, :], work[:, 0, :], ACT.Exp).then_inc(exp_done, 1)
                for n, (layer, b) in enumerate(flat):
                    s, w = POS_BLOCKS[b]
                    act.wait_ge(angle_ready, n + 1)
                    out = feats if layer == 0 else hidden
                    nc.scalar.activation(out[:, s:s + w], angle[:, n % 2, :w], ACT.Sin).then_inc(sine_done, 1)

            @block.vector
            def _(dve):
                own = Steps(dve, dve_step)
                a0, a1 = PARAMS["rg_a"]
                a = params[:, a0:a0 + a1]
                dve.wait_ge(loaded, 64)
                own.done(nc.vector.scalar_tensor_tensor(out=work[:, 0, :], in0=a, scalar=-1.0, in1=a,
                                                        op0=ALU.mult, op1=ALU.min))
                dve.wait_ge(exp_done, 1)
                own.done(nc.vector.tensor_scalar(work[:, 2, :], work[:, 1, :], 2.0, None, ALU.add))
                own.wait()
                own.done(nc.vector.reciprocal(work[:, 3, :], work[:, 2, :]))
                own.wait()
                own.done(nc.vector.tensor_tensor(work[:, 2, :], work[:, 1, :], work[:, 3, :], ALU.mult))
                own.wait()
                own.done(nc.vector.tensor_tensor(work[:, 3, :], work[:, 2, :], work[:, 2, :], ALU.mult))
                own.done(nc.vector.memset(work[:, 4, :], 1.0 / 19))
                own.wait()
                for odd in range(17, 0, -2):
                    own.done(nc.vector.tensor_tensor(work[:, 4, :], work[:, 4, :], work[:, 3, :], ALU.mult))
                    own.wait()
                    own.done(nc.vector.tensor_scalar(work[:, 4, :], work[:, 4, :], 1.0 / odd, None, ALU.add))
                    own.wait()
                own.done(nc.vector.scalar_tensor_tensor(out=work[:, 4, :], in0=work[:, 4, :], scalar=2.0,
                                                        in1=work[:, 2, :], op0=ALU.mult, op1=ALU.mult))
                own.done(nc.vector.tensor_scalar(work[:, 5, :], a, -1.0, 0.0, ALU.mult, ALU.max))
                own.wait()
                own.done(nc.vector.tensor_tensor(work[:, 5, :], work[:, 5, :], work[:, 4, :], ALU.add))
                own.wait()
                own.done(nc.vector.tensor_scalar(sp8[:], work[:, 5, :], RG_C, None, ALU.mult))
                own.done(nc.vector.tensor_scalar(nsp8[:], work[:, 5, :], -RG_C, None, ALU.mult))
                b0, f0 = PARAMS["mlp_b"][0], PARAMS["mlp_f"][0]
                own.done(nc.vector.tensor_tensor(bf[:], params[:, b0:b0 + 2], params[:, f0:f0 + 2], ALU.mult))
                own.wait()

                def reduce_angle(n, layer, b):
                    s, w = POS_BLOCKS[b]
                    x, k = angle[:, n % 2, :w], turns[:, n % 2, :w]
                    step = Steps(dve, angle_step, n * (sine_steps - 1))
                    dve.wait_ge(mlp_mm, n + 1)
                    if n >= 2:
                        dve.wait_ge(sine_done, n - 1)
                    step.done(nc.vector.tensor_scalar(x, ps_mlp[:, n % 4, :w], params[:, f0 + layer:f0 + layer + 1],
                                                      bf[:, layer:layer + 1], ALU.mult, ALU.add))
                    step.wait()
                    step.done(nc.vector.tensor_scalar(k, x, 1 / (2 * math.pi), round_magic, ALU.mult, ALU.add))
                    step.wait()
                    step.done(nc.vector.tensor_scalar(k, k, -round_magic, None, ALU.add))
                    step.wait()
                    step.done(nc.vector.scalar_tensor_tensor(out=x, in0=k, scalar=-two_pi_hi, in1=x,
                                                             op0=ALU.mult, op1=ALU.add))
                    step.wait()
                    assert step.n == sine_steps - 1
                    nc.vector.scalar_tensor_tensor(out=x, in0=k, scalar=-two_pi_lo, in1=x,
                                                   op0=ALU.mult, op1=ALU.add).then_inc(turns_done, 1)
                    dve.wait_ge(turns_done, n + 1)
                    nc.vector.tensor_scalar(x, x, pi_below, -pi_below, ALU.min, ALU.max).then_inc(angle_ready, 1)

                n = 0
                for c in range(chunks):
                    dve.wait_ge(chunk_done, c + 1)
                    at = c * width
                    nc.vector.tensor_tensor(rows[:, at:at + width], ps[:, c % 2, :], bias[:, at:at + width],
                                            ALU.add).then_inc(row_done, 1)
                    for layer, b in mlp_order[c]:
                        reduce_angle(n, layer, b)
                        n += 1
                dve.wait_ge(turn_done, 1)
                own.done(nc.vector.tensor_copy(mod[:], turned[:]))
                own.wait()
                for scale, at, g in ((scale1, SCALE1, "g1"), (scale2, SCALE2, "g2")):
                    g0, gw = PARAMS[g]
                    gain = params[:, g0:g0 + gw].unsqueeze(2).broadcast_to([P, KM, 2])
                    own.done(nc.vector.scalar_tensor_tensor(out=scale[:], in0=mod[:, at:at + KM, :], scalar=1.0,
                                                            in1=gain, op0=ALU.add, op1=ALU.mult))

            @block.gpsimd
            def _(pool):
                nc.gpsimd.memset(w1[:], 0.0).then_inc(mlp_zeroed, 1)
                nc.gpsimd.memset(w2[:], 0.0).then_inc(mlp_zeroed, 1)
                nc.gpsimd.memset(ones[:], 1.0).then_inc(ones_done, 1)
                nc.gpsimd.memset(keep["zero"][:], 0.0).then_inc(ones_done, 1)
                pool.wait_ge(ones_done, 2)

            @block.tensor
            def _(pe):
                pe.wait_ge(silu_done, 1)
                n = 0
                for c in range(chunks):
                    for layer, b in mlp_order[c]:
                        s, w = POS_BLOCKS[b]
                        if n == 0:
                            pe.wait_ge(mlp_loaded, 32)
                            pe.wait_ge(feats_loaded, 16)
                        if layer == 1:
                            pe.wait_ge(sine_done, flat.index((0, b)) + 1)
                        if n >= 4:
                            pe.wait_ge(angle_step, (n - 4) * (sine_steps - 1) + 1)
                        pe.matmul(ps_mlp[:, n % 4, :w], (w2 if layer else w1)[:], feats[:, s:s + w],
                                  start=True, stop=True).then_inc(mlp_mm, 1)
                        n += 1
                    pe.wait_ge(w_loaded[c % 3], c // 3 * 16 + 16)
                    if c >= 2:
                        pe.wait_ge(row_done, c - 1)
                    for k in range(KM):
                        last = pe.matmul(ps[:, c % 2, :], act_c[:, k, :], wada[:, c % 3, k, :],
                                         start=(k == 0), stop=(k == KM - 1))
                    last.then_inc(chunk_done, 1)
                pe.wait_ge(row_done, chunks)
                for j in range(N_MOD * KM):
                    last = pe.transpose(turned[:, j, :], rows[:, j * P:(j + 1) * P], ident[0:2, 0:2])
                last.then_inc(turn_done, 1)


def in_proj(nc, sem, d, keep):
    with ExitStack() as ctx:
        def sb(name, shape, dt=F32):
            return ctx.enter_context(nc.sbuf_tensor(name, shape, dt))

        def psum(name, shape, dt=F32):
            return ctx.enter_context(nc.psum_tensor(name, shape, dt))

        xh, xl = sb("xh", [P, KM, T], F32R), sb("xl", [P, KM, T], F32R)
        nb = norm_buffers(sb, psum, keep["norm_sems"], "in", 1)
        wb = weight_buffers(sb, sem, keep["zero"], "in")
        padded = sb("padded", [P, PAD_LEN])
        result = sb("in_result", [P, T])
        banks = psum("in_banks", [P, NB, 512])
        bank_free, pads_zero, tap_done, result_ready, result_stored = (sem(x) for x in (
            "in_bank_free", "in_pads_zero", "in_tap_done", "in_result_ready", "in_result_stored"))
        params, ones = keep["params"], keep["ones"]
        shift = keep["mod"][:, SHIFT1:SHIFT1 + KM, :]
        cw0, cb0 = PARAMS["cw"][0], PARAMS["cb"][0]

        with nc.Block() as block:
            @block.sync
            def _(sp):
                sp.dma_start(wb["whole"][:], d["w_in"][0]).then_inc(wb["loaded"], 16)
                norm_loads(sp, nb, d["xT"])
                sp.wait_ge(wb["ready"], 1)
                sp.dma_start(wb["whole"][:], d["w_in"][1]).then_inc(wb["loaded"], 16)
                with sp.Fori(2, N_IN) as n:
                    sp.wait_ge(wb["ready"], n)
                    sp.dma_start(wb["whole"][:], d["w_in"][n]).then_inc(wb["loaded"], 16)
                    sp.wait_ge(result_ready, n - 1)
                    sp.dma_start(d["pre"][n - 2], result[:]).then_inc(result_stored, 16)
                for n in range(N_IN - 2, N_IN):
                    sp.wait_ge(result_ready, n + 1)
                    sp.dma_start(d["pre"][n], result[:]).then_inc(result_stored, 16)
                sp.wait_ge(result_stored, 16 * (N_IN + 1))

            @block.scalar
            def _(act):
                norm_scalar(nc, act, nb, shift, xh)
                act.sem_inc(bank_free, NB)
                act.wait_ge(pads_zero, 1)
                with act.Fori(0, N_CONV) as n:
                    for b, (s, w) in enumerate(TOKEN_BLOCKS):
                        act.wait_ge(wb["block_done"], n * NB + b + 1)
                        for at, width, m in segments(s, w):
                            to = at + (PAD_AT_LAT if m == LAT else PAD_AT_CTX - CTX_AT)
                            last = nc.scalar.activation(padded[:, to:to + width], banks[:, b, at - s:at - s + width],
                                                        ACT.Copy)
                        last.then_inc(bank_free, 1)
                    act.wait_ge(result_ready, n + 1)
                with act.Fori(N_CONV, N_IN) as n:
                    act.wait_ge(result_stored, n * 16 + 16)
                    for b, (s, w) in enumerate(TOKEN_BLOCKS):
                        act.wait_ge(wb["block_done"], n * NB + b + 1)
                        nc.scalar.activation(result[:, s:s + w], banks[:, b, :w],
                                             ACT.Gelu_apprx_tanh).then_inc(bank_free, 1)
                    act.wait_ge(bank_free, n * NB + 2 * NB)
                    act.sem_inc(result_ready, 1)

            @block.vector
            def _(dve):
                nc.vector.memset(padded[:], 0.0).then_inc(pads_zero, 1)
                norm_vector(nc, dve, nb, keep["scale1"], shift, xh, xl)
                dve.sem_inc(result_stored, 16)
                with dve.Fori(0, N_CONV) as n:
                    own = Steps(dve, tap_done, n * 3)
                    dve.wait_ge(bank_free, n * NB + 2 * NB)
                    dve.wait_ge(result_stored, n * 16 + 16)
                    for tap in range(4):
                        weight = params[:, bass.ds(n * 4 + (cw0 + tap), 1)]
                        for to, at, width in ((0, 0, SEQ_LAT), (CTX_AT, PAD_AT_CTX - PAD_AT_LAT, SEQ_CTX)):
                            x, y = padded[:, at + tap:at + tap + width], result[:, to:to + width]
                            if tap == 0:
                                last = nc.vector.tensor_scalar(y, x, weight, params[:, bass.ds(n + cb0, 1)],
                                                               ALU.mult, ALU.add)
                            else:
                                last = nc.vector.scalar_tensor_tensor(out=y, in0=x, scalar=weight, in1=y,
                                                                      op0=ALU.mult, op1=ALU.add)
                        if tap < 3:
                            own.done(last)
                            own.wait()
                        else:
                            last.then_inc(result_ready, 1)

            @block.gpsimd
            def _(pool):
                weight_splits(nc, pool, wb, N_IN)

            @block.tensor
            def _(pe):
                norm_tensor(pe, nb, ones)
                with pe.Fori(0, N_IN // 2) as pair:
                    for u in range(2):
                        n = pair * 2 + u
                        pe.wait_ge(wb["ready"], n + 1)
                        for b, (s, w) in enumerate(TOKEN_BLOCKS):
                            norm_wait(pe, nb, "lo_ready", KM * (b + 1))
                            pe.wait_ge(bank_free, n * NB + b + 1)
                            product_block(pe, banks[:, b, :w], wb, u, xh, xl, s, w)


def rglru(nc, sem, d, keep):
    with ExitStack() as ctx:
        def sb(name, shape, dt=F32):
            return ctx.enter_context(nc.sbuf_tensor(name, shape, dt))

        gate_w = sb("gate_w", [P, 4 * CT, P])
        x, gy = sb("rg_x", [P, 2, T]), sb("rg_gelu_y", [P, 2, T])
        r, i, a, s2 = (sb(name, [P, 2, T]) for name in ("rg_r", "rg_i", "rg_a", "rg_s"))
        states = sb("rg_states", [P, CT, 2])
        banks = ctx.enter_context(nc.psum_tensor("rg_banks", [P, 8, 512], F32))
        zeroed, w_loaded, gate_mm, gate_done = (sem(q) for q in ("rg_zeroed", "rg_w_loaded", "rg_gate_mm", "rg_gate_done"))
        x_loaded, y_loaded = [sem("rg_x_loaded0"), sem("rg_x_loaded1")], [sem("rg_y_loaded0"), sem("rg_y_loaded1")]
        decay_done, one_minus, root_done, gated, input_ready, scanned, summed, out_ready, stored, state_done = (
            sem("rg_" + q) for q in ("decay_done", "one_minus", "root_done", "gated", "input_ready", "scanned",
                                     "summed", "out_ready", "stored", "state_done"))
        params = keep["params"]
        gb0, h00 = PARAMS["gate_b"][0], PARAMS["h0"][0]

        with nc.Block() as block:
            @block.sync
            def _(sp):
                sp.wait_ge(zeroed, 1)
                for half in range(2):
                    q = slice(64 * half, 64 * half + 64)
                    sp.dma_start(gate_w[q, :, q], d["gate_w"][half]).then_inc(w_loaded, 16)
                for ct in range(CT):
                    if ct >= 2:
                        sp.wait_ge(out_ready, ct - 1)
                    sp.dma_start(x[:, ct % 2], d["pre"][ct]).then_inc(x_loaded[ct % 2], 16)
                    sp.dma_start(gy[:, ct % 2], d["pre"][N_CONV + ct]).then_inc(y_loaded[ct % 2], 16)
                    if ct >= 1:
                        sp.wait_ge(out_ready, ct)
                        sp.dma_start(d["mixed"][ct - 1], i[:, 0]).then_inc(stored, 16)
                sp.wait_ge(out_ready, CT)
                sp.dma_start(d["mixed"][CT - 1], i[:, 0]).then_inc(stored, 16)
                sp.wait_ge(state_done, 2 * CT)
                sp.dma_start(d["states"], states[:]).then_inc(stored, 16)
                sp.wait_ge(stored, 16 * (CT + 1))

            @block.tensor
            def _(pe):
                pe.wait_ge(w_loaded, 32)
                for ct in range(CT):
                    pe.wait_ge(x_loaded[ct % 2], ct // 2 * 16 + 16)
                    for dg in range(4):
                        for b, (s, w) in enumerate(TOKEN_BLOCKS):
                            n = (ct * 4 + dg) * NB + b
                            if n >= 8:
                                pe.wait_ge(gate_done, n - 7)
                            pe.matmul(banks[:, n % 8, :w], gate_w[:, dg * CT + ct, :], x[:, ct % 2, s:s + w],
                                      start=True, stop=True).then_inc(gate_mm, 1)

            @block.scalar
            def _(act):
                for ct in range(CT):
                    if ct:
                        act.wait_ge(stored, 16 * ct)
                    for dg in range(4):
                        direction, gate = dg // 2, dg % 2
                        for b, (s, w) in enumerate(TOKEN_BLOCKS):
                            n = (ct * 4 + dg) * NB + b
                            act.wait_ge(gate_mm, n + 1)
                            nc.scalar.activation((r, i)[gate][:, direction, s:s + w], banks[:, n % 8, :w], ACT.Sigmoid,
                                                 bias=params[:, gb0 + dg * CT + ct:gb0 + dg * CT + ct + 1])\
                              .then_inc(gate_done, 1)
                    act.wait_ge(gate_done, (ct + 1) * 4 * NB)
                    for direction in range(2):
                        at = direction * CT + ct
                        n = 2 * ct + direction
                        nc.scalar.activation(a[:, direction], r[:, direction], ACT.Exp,
                                             scale=keep["nsp8"][:, at:at + 1]).then_inc(decay_done, 1)
                        act.wait_ge(decay_done, 3 * n + 1)
                        nc.scalar.activation(r[:, direction], r[:, direction], ACT.Tanh,
                                             scale=keep["sp8"][:, at:at + 1]).then_inc(decay_done, 1)
                        nc.scalar.activation(s2[:, direction], a[:, direction], ACT.Square).then_inc(decay_done, 1)
                    for direction in range(2):
                        act.wait_ge(one_minus, 2 * ct + direction + 1)
                        nc.scalar.activation(s2[:, direction], s2[:, direction], ACT.Sqrt).then_inc(root_done, 1)

            @block.gpsimd
            def _(pool):
                nc.gpsimd.memset(gate_w[:], 0.0).then_inc(zeroed, 1)

            @block.vector
            def _(dve):
                for ct in range(CT):
                    dve.wait_ge(x_loaded[ct % 2], ct // 2 * 16 + 16)
                    dve.wait_ge(y_loaded[ct % 2], ct // 2 * 16 + 16)
                    for direction in range(2):
                        n = 2 * ct + direction
                        dve.wait_ge(decay_done, 3 * n + 3)
                        nc.vector.scalar_tensor_tensor(out=s2[:, direction], in0=s2[:, direction], scalar=1.0,
                                                       in1=r[:, direction], op0=ALU.add, op1=ALU.mult)\
                          .then_inc(one_minus, 1)
                    for direction in range(2):
                        n = 2 * ct + direction
                        nc.vector.tensor_tensor(i[:, direction], i[:, direction], x[:, ct % 2], ALU.mult)\
                          .then_inc(gated, 1)
                        dve.wait_ge(gated, n + 1)
                        dve.wait_ge(root_done, n + 1)
                        nc.vector.tensor_tensor(s2[:, direction], s2[:, direction], i[:, direction], ALU.mult)\
                          .then_inc(input_ready, 1)
                        dve.wait_ge(input_ready, n + 1)
                        h0 = params[:, h00 + direction * CT + ct:h00 + direction * CT + ct + 1]
                        for lo, hi, start in ((0, CTX_AT, h0), (CTX_AT, T, 0.0)):
                            views = [t[:, direction, lo:hi] for t in (i, a, s2)]
                            if direction:
                                views = [v[:, ::-1] for v in views]
                            nc.vector.tensor_tensor_scan(*views, start, ALU.mult, ALU.add).then_inc(scanned, 1)
                        dve.wait_ge(scanned, 2 * n + 2)
                        end = T - 1 if direction == 0 else CTX_AT
                        nc.vector.tensor_copy(states[:, ct, direction:direction + 1], i[:, direction, end:end + 1])\
                          .then_inc(state_done, 1)
                    dve.wait_ge(state_done, 2 * ct + 2)
                    nc.vector.tensor_tensor(i[:, 0], i[:, 0], i[:, 1], ALU.add).then_inc(summed, 1)
                    dve.wait_ge(summed, ct + 1)
                    nc.vector.tensor_tensor(i[:, 0], i[:, 0], gy[:, ct % 2], ALU.mult).then_inc(out_ready, 1)

def interleave(*lists):
    keyed = [((i + 0.5) / len(x), n, i) for n, x in enumerate(lists) for i in range(len(x))]
    return [lists[n][i] for _, n, i in sorted(keyed)]


CONV_FORWARD = ([("turn_rows", j) for j in range(4)] + [("first", j) for j in range(8)]
                + [("turn_back", j) for j in range(8)] + [("second", j) for j in range(8)])
CONV_BACK = ([("back1", j) for j in range(8)] + [("turn_pairs", j) for j in range(8)]
             + [("back2", j) for j in range(4)])
FILTER_FIRST = [x for j in range(8) for x in (("taps", j), ("f_first", j))]
FILTER_SECOND = [x for j in range(8) for x in (("f_turn_back", j), ("f_second", j))]
CTX_FORWARD = [("ctx_turn", 0), ("ctx_forward", 0)]
CTX_BACK = [("ctx_back", 0)]
CTX_TAPS, CTX_FILTER = [("ctx_taps", 0)], [("ctx_filter", 0)]
BATCHES = {"turn_rows": 4, "first": 8, "turn_back": 8, "second": 8, "back1": 8, "turn_pairs": 8, "back2": 4,
           "taps": 8, "f_first": 8, "f_turn_back": 8, "f_second": 8,
           "ctx_turn": 1, "ctx_forward": 1, "ctx_back": 1, "ctx_taps": 1, "ctx_filter": 1}
ONLY_FILTER = FILTER_FIRST[:8] + CTX_TAPS + FILTER_FIRST[8:] + FILTER_SECOND + CTX_FILTER
ONLY_CONV = interleave(CONV_FORWARD, CTX_FORWARD) + interleave(CONV_BACK, CTX_BACK)
BOTH = (interleave(CONV_FORWARD, FILTER_FIRST, [CTX_FORWARD[0], CTX_TAPS[0], CTX_FORWARD[1]])
        + interleave(CONV_BACK, FILTER_SECOND, [CTX_BACK[0], CTX_FILTER[0]]))
CONV_CHAIN = CONV_FORWARD + CONV_BACK


def hyena(nc, sem, d, keep):
    with ExitStack() as ctx:
        def sb(name, shape, dt=F32):
            return ctx.enter_context(nc.sbuf_tensor(name, shape, dt))

        hidden = sb("hy_hidden", [P, POS])
        first_t, second_t = sb("first_table", [P, 2, 256]), sb("second_table", [P, 32, P])
        back1_t, back2_t = sb("back1_table", [P, 32, P]), sb("back2_table", [P, 64])
        ctx_fwd, ctx_inv = sb("ctx_forward_table", [P, 2, 2, P]), sb("ctx_back_table", [P, 2, P])
        decay = sb("decay", [P, ROW_TILES, P])
        w3 = sb("mlp_w3", [P, 2, 2, P])
        z = sb("hy_z", [P, T])
        gates = sb("hy_gates", [P, 2, T])
        rows = sb("hy_rows", [P, 16, P])
        spectrum_c = sb("hy_by_channel", [P, 64, 64])
        spectrum_p = sb("hy_by_slot", [P, 32, P])
        swapped = sb("hy_swapped", [P, 2, 4, P])
        gated = rows[:, 0:8].rearrange("p (j q) c -> p j (q c)", j=2)
        taps = sb("taps", [P, 2, 4, P])
        f_by_channel = sb("f_by_channel", [P, 64, 64])
        f_by_slot = sb("f_by_slot", [P, 2, 4, P])
        f_re, f_im = sb("filter_re", [P, 32, P]), sb("filter_im", [P, 32, P])
        ctx_rows, ctx_y, ctx_tmp = sb("ctx_rows", [P, P]), sb("ctx_y", [P, 2, P]), sb("ctx_tmp", [P, 2, P])
        ctx_taps, ctx_f = sb("ctx_taps", [P, 2, P]), sb("ctx_f", [P, 3, P])
        conv_bank = ctx.enter_context(nc.psum_tensor("conv_bank", [P, 4, 512], F32))
        filter_bank = ctx.enter_context(nc.psum_tensor("filter_bank", [P, 2, 512], F32))
        ctx_bank = ctx.enter_context(nc.psum_tensor("ctx_bank", [P, 2, 512], F32))

        mm = {q: sem(f"{q}_mm") for q in BATCHES}
        out = {q: sem(f"{q}_out") for q in BATCHES}
        tables_loaded, w3_zeroed = sem("hy_tables_loaded"), sem("w3_zeroed")
        z_loaded, gates_loaded, z_stored = sem("hy_z_loaded"), sem("hy_gates_loaded"), sem("hy_z_stored")
        decay_loaded, w3_loaded = sem("decay_loaded"), sem("w3_loaded")
        swap_ready, cross_ready, slots_ready = sem("swap_ready"), sem("cross_ready"), sem("slots_ready")
        re_ready, im_step = sem("filter_re_ready"), sem("filter_im_step")
        biased, ctx_step, ctx_biased, ctx_copied = (sem(q) for q in ("hy_biased", "ctx_step", "ctx_biased", "ctx_copied"))
        params, ident = keep["params"], keep["ident"]
        hb0 = PARAMS["hy_b"][0]

        def each_turn(engine, batch, both=True):
            for stage, j in ONLY_FILTER:
                batch(stage, j, 0, 0, None, 0)
            with engine.Fori(0, CT - 1) as ct:
                for order in range(2):
                    for stage, j in BOTH:
                        batch(stage, j, ct, order, ct * 2 + order, ct * 2 + (order + 1))
            for order in range(2):
                for stage, j in (BOTH, ONLY_CONV)[order]:
                    batch(stage, j, CT - 1, order, 2 * (CT - 1) + order, 2 * (CT - 1) + order + 1)

        with nc.Block() as block:
            @block.sync
            def _(sp):
                def load_filter_inputs(ct):
                    sp.dma_start(decay[:], d["decay"][ct]).then_inc(decay_loaded, 16)
                    for order in range(2):
                        sp.dma_start(w3[0:64, order], d["mlp_w3"][order][ct]).then_inc(w3_loaded, 16)

                def load_conv_inputs(ct):
                    sp.dma_start(z[:], d["pre"][ct + CT]).then_inc(z_loaded, 16)
                    for order in range(2):
                        sp.dma_start(gates[:, order], d["pre"][ct + (2 + order) * CT]).then_inc(gates_loaded, 16)

                sp.wait_ge(w3_zeroed, 1)
                sp.dma_start(hidden[:], d["hidden"]).then_inc(tables_loaded, 16)
                load_filter_inputs(0)
                for dst, src in ((first_t, "first_table"), (second_t, "second_table"), (ctx_fwd, "ctx_forward_table"),
                                 (back1_t, "back1_table"), (back2_t, "back2_table"), (ctx_inv, "ctx_back_table")):
                    sp.dma_start(dst[:], d[src]).then_inc(tables_loaded, 16)
                load_conv_inputs(0)

                def finish(ct):
                    sp.wait_ge(out["back2"], ct * 8 + 8)
                    sp.wait_ge(out["ctx_back"], ct * 2 + 2)
                    sp.dma_start(d["mixed"][ct + CT], z[:]).then_inc(z_stored, 16)

                with sp.Fori(0, CT - 1) as ct:
                    sp.wait_ge(out["taps"], ct * 16 + 16)
                    sp.wait_ge(out["ctx_taps"], ct * 2 + 2)
                    load_filter_inputs(ct + 1)
                    finish(ct)
                    sp.wait_ge(z_stored, ct * 16 + 16)
                    load_conv_inputs(ct + 1)
                finish(CT - 1)
                sp.wait_ge(z_stored, 16 * CT)

            @block.tensor
            def _(pe):
                def batch(stage, j, ct, order, turn, f_turn):
                    if (stage, j) in CONV_CHAIN:
                        at = CONV_CHAIN.index((stage, j))
                        bank = conv_bank[:, at % 4, :]
                        if at >= 4:
                            before, jb = CONV_CHAIN[at - 4]
                            pe.wait_ge(out[before], turn * BATCHES[before] + jb + 1)
                    four = lambda t: t.rearrange("p (q c) -> p q c", q=4)
                    if stage == "turn_rows":
                        if j == 0:
                            if order == 0:
                                pe.wait_ge(z_loaded, ct * 16 + 16)
                            else:
                                pe.wait_ge(out["back2"], turn * 4)
                        for q in range(4):
                            last = pe.transpose(four(bank)[:, q], z[:, 4 * j + q:SEQ_LAT:16], ident[:])
                    elif stage == "first":
                        pe.wait_ge(out["turn_rows"], turn * 4 + j // 2 + 1)
                        for q in range(2):
                            last = pe.matmul(bank[:, 256 * q:256 * q + 256], rows[:, 2 * j + q], first_t[:, 0],
                                             start=True, stop=True)
                    elif stage == "turn_back":
                        if j == 0:
                            pe.wait_ge(out["first"], turn * 8 + 8)
                        for q in range(4):
                            g = 4 * j + q
                            last = pe.transpose(four(bank)[:, q], spectrum_c[:, 2 * g:2 * g + 2, :]
                                                .rearrange("p r b -> p (r b)"), ident[:])
                    elif stage == "second":
                        pe.wait_ge(out["turn_back"], turn * 8 + j + 1)
                        for q in range(4):
                            g = 4 * j + q
                            last = pe.matmul(four(bank)[:, q], second_t[:, g], spectrum_p[:, g], start=True, stop=True)
                    elif stage == "back1":
                        pe.wait_ge(slots_ready, turn * 8 + j + 1)
                        for q in range(4):
                            g = 4 * j + q
                            last = pe.matmul(four(bank)[:, q], spectrum_p[:, g], back1_t[:, g], start=True, stop=True)
                    elif stage == "turn_pairs":
                        if j == 0:
                            pe.wait_ge(out["back1"], turn * 8 + 8)
                        flat = spectrum_c[:].rearrange("p r b -> p (r b)")
                        for q in range(4):
                            g = 4 * j + q
                            last = pe.transpose(four(bank)[:, q], flat[:, g:4096:32], ident[:])
                    elif stage == "back2":
                        pe.wait_ge(out["turn_pairs"], turn * 8 + 2 * j + 2)
                        for q in range(8):
                            last = pe.matmul(bank[:, 64 * q:64 * q + 64], spectrum_p[:, 8 * j + q], back2_t[:],
                                             start=True, stop=True)
                    elif stage == "taps":
                        if j == 0:
                            pe.wait_ge(w3_loaded, f_ct(order, turn, ct) * 32 + 32)
                            if turn is None:
                                pe.wait_ge(tables_loaded, 16 * 7)
                            else:
                                pe.wait_ge(out["f_turn_back"], f_turn * 8)
                        else:
                            pe.wait_ge(out["taps"], f_turn * 8 + j)
                        for q in range(4):
                            rt = 4 * j + q
                            last = pe.matmul(four(filter_bank[:, 0])[:, q], hidden[:, rt * P:rt * P + P],
                                             w3[:, f_order(order, turn), q % 2], start=True, stop=True)
                    elif stage == "f_first":
                        pe.wait_ge(out["taps"], f_turn * 8 + j + 1)
                        if j == 0 and turn is not None:
                            pe.wait_ge(out["f_second"], f_turn * 8)
                        elif j:
                            pe.wait_ge(out["f_first"], f_turn * 8 + j)
                        for q in range(2):
                            for half in range(2):
                                last = pe.matmul(filter_bank[:, 1, 256 * q:256 * q + 256], taps[:, j % 2, 2 * q + half],
                                                 first_t[:, half], start=(half == 0), stop=(half == 1))
                    elif stage == "f_turn_back":
                        if j == 0:
                            pe.wait_ge(out["f_first"], f_turn * 8 + 8)
                            pe.wait_ge(out["taps"], f_turn * 8 + 8)
                        else:
                            pe.wait_ge(out["f_turn_back"], f_turn * 8 + j)
                        for q in range(4):
                            g = 4 * j + q
                            last = pe.transpose(four(filter_bank[:, 0])[:, q], f_by_channel[:, 2 * g:2 * g + 2, :]
                                                .rearrange("p r b -> p (r b)"), ident[:])
                    elif stage == "f_second":
                        pe.wait_ge(out["f_turn_back"], f_turn * 8 + j + 1)
                        if j:
                            pe.wait_ge(out["f_second"], f_turn * 8 + j)
                        for q in range(4):
                            last = pe.matmul(four(filter_bank[:, 1])[:, q], second_t[:, 4 * j + q], f_by_slot[:, j % 2, q],
                                             start=True, stop=True)
                    elif stage == "ctx_turn":
                        if order == 0:
                            pe.wait_ge(z_loaded, ct * 16 + 16)
                        else:
                            pe.wait_ge(out["ctx_back"], turn)
                        pe.wait_ge(out["ctx_filter"], turn + 1)
                        last = pe.transpose(ctx_bank[:, 0, :P], z[:, CTX_AT:T], ident[:])
                    elif stage == "ctx_forward":
                        pe.wait_ge(out["ctx_turn"], turn + 1)
                        for part in range(2):
                            last = pe.matmul(ctx_bank[:, 0, P * part:P * part + P], ctx_fwd[:, 0, part], ctx_rows[:],
                                             start=True, stop=True)
                    elif stage == "ctx_back":
                        pe.wait_ge(out["ctx_forward"], turn + 1)
                        pe.wait_ge(out["ctx_taps"], turn + 1)
                        for part in range(2):
                            last = pe.matmul(ctx_bank[:, 1, :P], ctx_y[:, part], ctx_inv[:, part],
                                             start=(part == 0), stop=(part == 1))
                    elif stage == "ctx_taps":
                        if order == 1:
                            pe.wait_ge(out["ctx_back"], turn)
                        for half in range(2):
                            last = pe.matmul(ctx_bank[:, 1, P * half:P * half + P],
                                             hidden[:, POS_LAT + half * P:POS_LAT + half * P + P],
                                             w3[:, f_order(order, turn), half], start=True, stop=True)
                    elif stage == "ctx_filter":
                        pe.wait_ge(out["ctx_taps"], f_turn + 1)
                        if turn is not None:
                            pe.wait_ge(out["ctx_forward"], turn + 1)
                        for part in range(2):
                            for half in range(2):
                                last = pe.matmul(ctx_bank[:, 0, P * part:P * part + P], ctx_fwd[:, half, part],
                                                 ctx_taps[:, half], start=(half == 0), stop=(half == 1))
                    last.then_inc(mm[stage], 1)

                each_turn(pe, batch)

            @block.scalar
            def _(act):
                def batch(stage, j, ct, order, turn, f_turn):
                    at = CONV_CHAIN.index((stage, j)) if (stage, j) in CONV_CHAIN else 0
                    bank = conv_bank[:, at % 4, :]
                    if stage == "turn_rows":
                        act.wait_ge(mm[stage], turn * 4 + j + 1)
                        nc.scalar.activation(rows[:, 4 * j:4 * j + 4].rearrange("p q c -> p (q c)"), bank,
                                             ACT.Copy).then_inc(out[stage], 1)
                    elif stage in ("first", "f_first"):
                        t, source, by_channel = ((turn, bank, spectrum_c) if stage == "first"
                                                 else (f_turn, filter_bank[:, 1], f_by_channel))
                        act.wait_ge(mm[stage], t * 8 + j + 1)
                        for q in range(2):
                            last = nc.scalar.activation(by_channel[:, :, 8 * j + 4 * q:8 * j + 4 * q + 4],
                                                        source[:, 256 * q:256 * q + 256].rearrange("p (r b) -> p r b", b=4),
                                                        ACT.Copy)
                        last.then_inc(out[stage], 1)
                    elif stage == "second":
                        act.wait_ge(mm[stage], turn * 8 + j + 1)
                        if j >= 2:
                            act.wait_ge(slots_ready, turn * 8 + j - 1)
                        to = swapped[:, j % 2].rearrange("p q c -> p (q c)")
                        nc.scalar.activation(to[0:64], bank[64:128], ACT.Copy)
                        nc.scalar.activation(to[64:128], bank[0:64], ACT.Copy).then_inc(swap_ready, 1)
                    elif stage == "back1":
                        act.wait_ge(mm[stage], turn * 8 + j + 1)
                        nc.scalar.activation(spectrum_c[:, 8 * j:8 * j + 8, :].rearrange("p r b -> p (r b)"), bank,
                                             ACT.Copy).then_inc(out[stage], 1)
                    elif stage == "f_second":
                        act.wait_ge(mm[stage], f_turn * 8 + j + 1)
                        to = f_re[:, 4 * j:4 * j + 4].rearrange("p q c -> p (q c)")
                        nc.scalar.activation(to[0:64], filter_bank[0:64, 1], ACT.Copy)
                        last = nc.scalar.activation(to[64:128], filter_bank[0:64, 1], ACT.Copy).then_inc(re_ready, 1)
                        if j == 0:
                            act.wait_ge(re_ready, f_turn * 9 + 1)
                            nc.scalar.activation(f_re[96:97, 0], filter_bank[96:97, 1, 0:P], ACT.Copy).then_inc(re_ready, 1)
                    elif stage == "ctx_turn":
                        act.wait_ge(mm[stage], turn + 1)
                        nc.scalar.activation(ctx_rows[:], ctx_bank[:, 0, :P], ACT.Copy).then_inc(out[stage], 1)
                    elif stage == "ctx_filter":
                        act.wait_ge(mm[stage], f_turn + 1)
                        nc.scalar.activation(ctx_f[:, 0], ctx_bank[:, 0, 0:P], ACT.Copy)
                        nc.scalar.activation(ctx_f[:, 1], ctx_bank[:, 0, P:2 * P], ACT.Copy)
                        nc.scalar.activation(ctx_f[:, 2], ctx_bank[:, 0, 0:P], ACT.Copy).then_inc(ctx_copied, 1)
                        act.wait_ge(ctx_copied, f_turn * 2 + 1)
                        nc.scalar.activation(ctx_f[0:1, 2], ctx_f[0:1, 1], ACT.Copy).then_inc(ctx_copied, 1)
                        act.wait_ge(ctx_copied, f_turn * 2 + 2)
                        nc.scalar.activation(ctx_f[0:1, 1], ctx_f[0:1, 1], ACT.Copy, scale=0.0).then_inc(out[stage], 1)

                each_turn(act, batch)

            @block.gpsimd
            def _(pool):
                nc.gpsimd.memset(w3[:], 0.0).then_inc(w3_zeroed, 1)

                def batch(stage, j, ct, order, turn, f_turn):
                    if stage == "second":
                        pool.wait_ge(swap_ready, turn * 8 + j + 1)
                        nc.gpsimd.tensor_tensor(swapped[:, j % 2], swapped[:, j % 2], f_im[:, 4 * j:4 * j + 4],
                                                ALU.mult).then_inc(cross_ready, 1)
                    elif stage == "back2":
                        if j == 0:
                            pool.wait_ge(gates_loaded, ct * 32 + 32)
                        pool.wait_ge(biased, turn * 4 + j + 1)
                        at = slice(8 * j, 8 * j + 8)
                        view = lambda t: t.rearrange("p (m b) -> p m b", b=32)[:, :, at]
                        nc.gpsimd.tensor_tensor(view(z[:, :SEQ_LAT]), gated[:, j % 2].rearrange("p (m b) -> p m b", b=8),
                                                view(gates[:, order, :SEQ_LAT]), ALU.mult).then_inc(out[stage], 1)

                each_turn(pool, batch)

            @block.vector
            def _(dve):
                def batch(stage, j, ct, order, turn, f_turn):
                    at = CONV_CHAIN.index((stage, j)) if (stage, j) in CONV_CHAIN else 0
                    bank = conv_bank[:, at % 4, :]
                    bias = params[:, bass.ds(ct + (hb0 + order * CT), 1)]
                    flat4 = lambda t: t.rearrange("p q c -> p (q c)")
                    if stage in ("turn_back", "turn_pairs"):
                        dve.wait_ge(mm[stage], turn * 8 + j + 1)
                        nc.vector.tensor_copy(flat4(spectrum_p[:, 4 * j:4 * j + 4]), bank).then_inc(out[stage], 1)
                    elif stage == "second":
                        dve.wait_ge(swap_ready, turn * 8 + j + 1)
                        nc.vector.tensor_tensor(flat4(spectrum_p[:, 4 * j:4 * j + 4]), bank, flat4(f_re[:, 4 * j:4 * j + 4]),
                                                ALU.mult).then_inc(out[stage], 1)
                        dve.wait_ge(out[stage], turn * 8 + j + 1)
                        dve.wait_ge(cross_ready, turn * 8 + j + 1)
                        nc.vector.tensor_tensor(spectrum_p[:, 4 * j:4 * j + 4], spectrum_p[:, 4 * j:4 * j + 4],
                                                swapped[:, j % 2], ALU.add).then_inc(slots_ready, 1)
                    elif stage == "back2":
                        dve.wait_ge(mm[stage], turn * 4 + j + 1)
                        if j >= 2:
                            dve.wait_ge(out[stage], turn * 4 + j - 1)
                        nc.vector.scalar_tensor_tensor(
                            out=gated[:, j % 2].rearrange("p (m b) -> p m b", b=8),
                            in0=z[:, :SEQ_LAT].rearrange("p (m b) -> p m b", b=32)[:, :, 8 * j:8 * j + 8], scalar=bias,
                            in1=bank.rearrange("p (b m) -> p m b", b=8), op0=ALU.mult, op1=ALU.add).then_inc(biased, 1)
                    elif stage == "taps":
                        if j == 0:
                            dve.wait_ge(decay_loaded, f_ct(order, turn, ct) * 16 + 16)
                        dve.wait_ge(mm[stage], f_turn * 8 + j + 1)
                        if j >= 2:
                            dve.wait_ge(mm["f_first"], f_turn * 8 + j - 1)
                        nc.vector.tensor_tensor(flat4(taps[:, j % 2]), filter_bank[:, 0], flat4(decay[:, 4 * j:4 * j + 4]),
                                                ALU.mult).then_inc(out[stage], 1)
                    elif stage == "f_turn_back":
                        dve.wait_ge(mm[stage], f_turn * 8 + j + 1)
                        if j >= 2:
                            dve.wait_ge(mm["f_second"], f_turn * 8 + j - 1)
                        nc.vector.tensor_copy(flat4(f_by_slot[:, j % 2]), filter_bank[:, 0]).then_inc(out[stage], 1)
                    elif stage == "f_second":
                        dve.wait_ge(re_ready, f_turn * 9 + j + 2)
                        to = flat4(f_im[:, 4 * j:4 * j + 4])
                        nc.vector.tensor_copy(to[64:128], filter_bank[64:128, 1])
                        last = nc.vector.tensor_scalar(to[0:64], filter_bank[64:128, 1], -1.0, None, ALU.mult)
                        if j == 0:
                            last.then_inc(im_step, 1)
                            dve.wait_ge(im_step, f_turn * 2 + 1)
                            nc.vector.memset(f_im[32:33, 0], 0.0)
                            nc.vector.memset(f_im[96:97, 0], 0.0).then_inc(im_step, 1)
                            dve.wait_ge(im_step, f_turn * 2 + 2)
                            dve.sem_inc(out[stage], 1)
                        else:
                            last.then_inc(out[stage], 1)
                    elif stage == "ctx_taps":
                        dve.wait_ge(mm[stage], f_turn + 1)
                        nc.vector.tensor_tensor(flat4(ctx_taps[:]), ctx_bank[:, 1, 0:2 * P], flat4(decay[:, 32:34]),
                                                ALU.mult).then_inc(out[stage], 1)
                    elif stage == "ctx_forward":
                        dve.wait_ge(mm[stage], turn + 1)
                        u_re, u_im = ctx_bank[:, 0, 0:P], ctx_bank[:, 0, P:2 * P]
                        for part, (p, q, op) in enumerate(((0, 1, ALU.subtract), (1, 2, ALU.add))):
                            done = turn * 4 + 2 * part
                            nc.vector.tensor_tensor(ctx_y[:, part], u_re, ctx_f[:, p], ALU.mult)
                            nc.vector.tensor_tensor(ctx_tmp[:, part], u_im, ctx_f[:, q], ALU.mult).then_inc(ctx_step, 1)
                            dve.wait_ge(ctx_step, done + 1)
                            last = nc.vector.tensor_tensor(ctx_y[:, part], ctx_y[:, part], ctx_tmp[:, part], op)
                            last.then_inc(ctx_step, 1)
                        dve.wait_ge(ctx_step, turn * 4 + 4)
                        dve.sem_inc(out[stage], 1)
                    elif stage == "ctx_back":
                        dve.wait_ge(mm[stage], turn + 1)
                        dve.wait_ge(gates_loaded, ct * 32 + 32)
                        nc.vector.scalar_tensor_tensor(out=ctx_tmp[:, 0], in0=z[:, CTX_AT:], scalar=bias,
                                                       in1=ctx_bank[:, 1, :P], op0=ALU.mult, op1=ALU.add).then_inc(ctx_biased, 1)
                        dve.wait_ge(ctx_biased, turn + 1)
                        nc.vector.tensor_tensor(z[:, CTX_AT:], ctx_tmp[:, 0], gates[:, order, CTX_AT:],
                                                ALU.mult).then_inc(out[stage], 1)

                each_turn(dve, batch)


def f_order(order, turn):
    return 0 if turn is None else 1 - order


def f_ct(order, turn, ct):
    return 0 if turn is None else ct + order


def out_proj(nc, sem, d, keep):
    with ExitStack() as ctx:
        def sb(name, shape, dt=F32):
            return ctx.enter_context(nc.sbuf_tensor(name, shape, dt))

        def psum(name, shape, dt=F32):
            return ctx.enter_context(nc.psum_tensor(name, shape, dt))

        xh, xl = sb("oh", [P, KM, T], F32R), sb("ol", [P, KM, T], F32R)
        nb = norm_buffers(sb, psum, keep["norm_sems"], "out", 2)
        wb = weight_buffers(sb, sem, keep["zero"], "out")
        x = sb("residual", [P, 2, T])
        banks = psum("out_banks", [P, NB, 512])
        bank_free, added, stored = sem("out_bank_free"), sem("out_added"), sem("out_stored")
        x_loaded = [sem("residual_loaded0"), sem("residual_loaded1")]
        params, mod = keep["params"], keep["mod"]
        go0 = PARAMS["go"][0]
        gain = params[:, go0:go0 + KM].unsqueeze(2).broadcast_to([P, KM, 2])

        with nc.Block() as block:
            @block.sync
            def _(sp):
                sp.dma_start(wb["whole"][:], d["w_out"][0]).then_inc(wb["loaded"], 16)
                norm_loads(sp, nb, d["mixed"])
                for n in range(KM):
                    if n:
                        sp.wait_ge(wb["ready"], n)
                        sp.dma_start(wb["whole"][:], d["w_out"][n]).then_inc(wb["loaded"], 16)
                    if n >= 2:
                        sp.wait_ge(added, (n - 1) * NB)
                        sp.dma_start(d["x1"][n - 2], x[:, n % 2]).then_inc(stored, 16)
                        sp.wait_ge(stored, 16 * (n - 1))
                    sp.dma_start(x[:, n % 2], d["xT"][n]).then_inc(x_loaded[n % 2], 16)
                for n in (KM - 2, KM - 1):
                    sp.wait_ge(added, (n + 1) * NB)
                    sp.dma_start(d["x1"][n], x[:, n % 2]).then_inc(stored, 16)
                sp.wait_ge(stored, 16 * KM)

            @block.scalar
            def _(act):
                norm_scalar(nc, act, nb, None, xh)

            @block.gpsimd
            def _(pool):
                weight_splits(nc, pool, wb, KM)

            @block.tensor
            def _(pe):
                norm_tensor(pe, nb, keep["ones"])
                for n in range(KM):
                    pe.wait_ge(wb["ready"], n + 1)
                    for b, (s, w) in enumerate(TOKEN_BLOCKS):
                        if n == 0:
                            norm_wait(pe, nb, "lo_ready", KM * (b + 1))
                        else:
                            pe.wait_ge(added, (n - 1) * NB + b + 1)
                        product_block(pe, banks[:, b, :w], wb, n % 2, xh, xl, s, w)

            @block.vector
            def _(dve):
                norm_vector(nc, dve, nb, gain, None, xh, xl)
                for n in range(KM):
                    dve.wait_ge(x_loaded[n % 2], n // 2 * 16 + 16)
                    for b, (s, w) in enumerate(TOKEN_BLOCKS):
                        dve.wait_ge(wb["block_done"], n * NB + b + 1)
                        for at, width, m in segments(s, w):
                            last = nc.vector.scalar_tensor_tensor(
                                out=x[:, n % 2, at:at + width], in0=banks[:, b, at - s:at - s + width],
                                scalar=mod[:, GATE1 + n, m:m + 1], in1=x[:, n % 2, at:at + width],
                                op0=ALU.mult, op1=ALU.add)
                        last.then_inc(added, 1)


def ffn_up(nc, sem, d, keep):
    pitch = GRID_W + 2
    with ExitStack() as ctx:
        def sb(name, shape, dt=F32):
            return ctx.enter_context(nc.sbuf_tensor(name, shape, dt))

        def psum(name, shape, dt=F32):
            return ctx.enter_context(nc.psum_tensor(name, shape, dt))

        xh, xl = sb("xh2", [P, KM, T], F32R), sb("xl2", [P, KM, T], F32R)
        nb = norm_buffers(sb, psum, keep["norm_sems"], "up", 1)
        wb = weight_buffers(sb, sem, keep["zero"], "up")
        grid = sb("grid", [P, GRID_H + 2, pitch])
        line = sb("line", [P, SEQ_CTX + 2])
        h = sb("ffn_hidden", [P, T])
        gate_bank = psum("gate_bank", [P, 2, 512])
        factor_bank = psum("factor_bank", [P, NB, 512])
        borders_zero, gate_out, factor_free, tap_done, conv_ready, gelu_ready, h_ready, h_stored = (
            sem("up_" + q) for q in ("borders_zero", "gate_out", "factor_free", "tap_done", "conv_ready",
                                     "gelu_ready", "h_ready", "h_stored"))
        params = keep["params"]
        shift = keep["mod"][:, SHIFT2:SHIFT2 + KM, :]
        fw0, fb0 = PARAMS["ffn_w"][0], PARAMS["ffn_b"][0]
        taps = [(dy, dx) for dy in range(3) for dx in range(3)]

        with nc.Block() as block:
            @block.sync
            def _(sp):
                sp.dma_start(wb["whole"][:], d["w_up"][0]).then_inc(wb["loaded"], 16)
                norm_loads(sp, nb, d["x1"])
                sp.wait_ge(wb["ready"], 1)
                sp.dma_start(wb["whole"][:], d["w_up"][1]).then_inc(wb["loaded"], 16)
                with sp.Fori(1, KF) as f:
                    for u in range(2):
                        sp.wait_ge(wb["ready"], f * 2 + u)
                        sp.dma_start(wb["whole"][:], d["w_up"][f * 2 + u]).then_inc(wb["loaded"], 16)
                    sp.wait_ge(h_ready, f)
                    sp.dma_start(d["hidden_ff"][f - 1], h[:]).then_inc(h_stored, 16)
                sp.wait_ge(h_ready, KF)
                sp.dma_start(d["hidden_ff"][KF - 1], h[:]).then_inc(h_stored, 16)
                sp.wait_ge(h_stored, 16 * (KF + 1))

            @block.scalar
            def _(act):
                norm_scalar(nc, act, nb, shift, xh)
                act.sem_inc(gate_out, 2)
                act.wait_ge(borders_zero, 2)
                with act.Fori(0, KF) as f:
                    for b, (s, w) in enumerate(TOKEN_BLOCKS):
                        act.wait_ge(wb["block_done"], f * 2 * NB + b + 1)
                        for at, width, m in segments(s, w):
                            source = gate_bank[:, b % 2, at - s:at - s + width]
                            if m == LAT:
                                y = at // GRID_W + 1
                                last = nc.scalar.activation(grid[:, y:y + width // GRID_W, 1:1 + GRID_W],
                                                            source.rearrange("p (y x) -> p y x", x=GRID_W), ACT.Copy)
                            else:
                                last = nc.scalar.activation(line[:, 1:1 + SEQ_CTX], source, ACT.Copy)
                        last.then_inc(gate_out, 1)
                    act.wait_ge(conv_ready, f + 1)
                    nc.scalar.activation(h[:], h[:], ACT.Gelu_apprx_tanh).then_inc(gelu_ready, 1)

            @block.gpsimd
            def _(pool):
                nc.gpsimd.memset(grid[:], 0.0).then_inc(borders_zero, 1)
                nc.gpsimd.memset(line[:], 0.0).then_inc(borders_zero, 1)
                weight_splits(nc, pool, wb, 2 * KF)

            @block.vector
            def _(dve):
                norm_vector(nc, dve, nb, keep["scale2"], shift, xh, xl)
                dve.sem_inc(factor_free, NB)
                dve.sem_inc(h_stored, 16)
                with dve.Fori(0, KF) as f:
                    own = Steps(dve, tap_done, f * (len(taps) - 1))
                    dve.wait_ge(gate_out, f * NB + (2 + NB))
                    dve.wait_ge(h_stored, f * 16 + 16)
                    for n, (dy, dx) in enumerate(taps):
                        weight = params[:, bass.ds(f + (fw0 + n * KF), 1)]
                        y = h[:, :SEQ_LAT].rearrange("p (y x) -> p y x", x=GRID_W)
                        window = grid[:, dy:dy + GRID_H, dx:dx + GRID_W]
                        if n == 0:
                            last = nc.vector.tensor_scalar(y, window, weight, params[:, bass.ds(f + fb0, 1)],
                                                           ALU.mult, ALU.add)
                        else:
                            last = nc.vector.scalar_tensor_tensor(out=y, in0=window, scalar=weight, in1=y,
                                                                  op0=ALU.mult, op1=ALU.add)
                        if dy == 1:
                            y, window = h[:, CTX_AT:], line[:, dx:dx + SEQ_CTX]
                            if dx == 0:
                                last = nc.vector.tensor_scalar(y, window, weight, params[:, bass.ds(f + fb0, 1)],
                                                               ALU.mult, ALU.add)
                            else:
                                last = nc.vector.scalar_tensor_tensor(out=y, in0=window, scalar=weight, in1=y,
                                                                      op0=ALU.mult, op1=ALU.add)
                        if n < len(taps) - 1:
                            own.done(last)
                            own.wait()
                        else:
                            last.then_inc(conv_ready, 1)
                    dve.wait_ge(gelu_ready, f + 1)
                    for b, (s, w) in enumerate(TOKEN_BLOCKS):
                        dve.wait_ge(wb["block_done"], f * 2 * NB + (NB + b + 1))
                        nc.vector.tensor_tensor(h[:, s:s + w], h[:, s:s + w], factor_bank[:, b, :w],
                                                ALU.mult).then_inc(factor_free, 1)
                    dve.wait_ge(factor_free, f * NB + 2 * NB)
                    dve.sem_inc(h_ready, 1)

            @block.tensor
            def _(pe):
                norm_tensor(pe, nb, keep["ones"])
                with pe.Fori(0, KF) as f:
                    for u in range(2):
                        pe.wait_ge(wb["ready"], f * 2 + (u + 1))
                        for b, (s, w) in enumerate(TOKEN_BLOCKS):
                            if u == 0:
                                norm_wait(pe, nb, "lo_ready", KM * (b + 1))
                                pe.wait_ge(gate_out, f * NB + max(2, b + 1))
                                bank = gate_bank[:, b % 2, :w]
                            else:
                                pe.wait_ge(factor_free, f * NB + (b + 1))
                                bank = factor_bank[:, b, :w]
                            product_block(pe, bank, wb, u, xh, xl, s, w)


DOWN_W = 272
DOWN_BLOCKS = T // DOWN_W


def ffn_down(nc, sem, d, keep):
    with ExitStack() as ctx:
        def sb(name, shape, dt=F32):
            return ctx.enter_context(nc.sbuf_tensor(name, shape, dt))

        whole = sb("down_whole", [P, D_MODEL])
        wh, wl = sb("down_hi", [P, KF, D_MODEL], F32R), sb("down_lo", [P, KF, D_MODEL], F32R)
        h = sb("down_h", [P, 4, DOWN_W])
        hh, hl = sb("down_h_hi", [P, 2, DOWN_W], F32R), sb("down_h_lo", [P, 2, DOWN_W], F32R)
        x = sb("down_x", [P, KM, DOWN_W])
        square = sb("down_square", [P, DOWN_W])
        total, rstd = sb("down_total", [P, DOWN_W]), sb("down_rstd", [P, DOWN_W])
        banks = ctx.enter_context(nc.psum_tensor("down_banks", [P, KM, 512], F32))
        w_loaded, w_hi, w_ready = sem("down_w_loaded"), sem("down_w_hi"), sem("down_w_ready")
        h_loaded = [sem(f"down_h_loaded{slot}") for slot in range(4)]
        h_hi, h_ready, k_done, added, x_loaded = (sem("down_" + q) for q in ("h_hi", "h_ready", "k_done", "added", "x_loaded"))
        squared, summed, total_ready, inverse_step, root_ready, result_ready, stored = (
            sem("down_" + q) for q in ("squared", "summed", "total_ready", "inverse_step", "root_ready",
                                       "result_ready", "stored"))
        params, mod = keep["params"], keep["mod"]
        gf0 = PARAMS["gf"][0]

        def pieces(last_block):
            if not last_block:
                return [(0, DOWN_W, LAT)]
            start = (DOWN_BLOCKS - 1) * DOWN_W
            return [(s - start, w, m) for s, w, m in segments(start, DOWN_W)]

        slots = [k % 4 if k < 16 else (k - 16) % 3 for k in range(KF)]
        slot_turns = [slots.count(slot) for slot in range(4)]
        per_block = KF - 1 + KM

        def h_slot(k):
            return slots[k], slots[:k].count(slots[k])

        def rows_since(k):
            return next(back for back in range(1, KF) if slots[(k - back) % KF] == slots[k])

        def tokens(source, block):
            return source[:, bass.ds(block * DOWN_W, DOWN_W)]

        with nc.Block() as block_:
            @block_.sync
            def _(sp):
                def load_h(block, k):
                    slot = h_slot(k)[0]
                    sp.dma_start(h[:, slot], tokens(d["hidden_ff"][k], block)).then_inc(h_loaded[slot], 16)

                def load_x(block):
                    for m in range(KM):
                        sp.dma_start(x[:, m], tokens(d["x1"][m], block)).then_inc(x_loaded, 16)

                load_x(0)
                for k in range(KF):
                    if k:
                        sp.wait_ge(w_ready, k)
                    sp.dma_start(whole[:], d["w_down"][k]).then_inc(w_loaded, 16)
                    if k >= 4:
                        sp.wait_ge(h_ready, k - rows_since(k) + 1)
                    load_h(0, k)
                with sp.Fori(1, DOWN_BLOCKS) as block:
                    for k in range(KF):
                        sp.wait_ge(h_ready, block * KF + (k - rows_since(k) + 1))
                        load_h(block, k)
                        if k == KF // 2:
                            sp.wait_ge(result_ready, block * KM)
                            for m in range(KM):
                                sp.dma_start(tokens(d["y"][m], block - 1), x[:, m]).then_inc(stored, 16)
                            sp.wait_ge(stored, block * (16 * KM))
                            load_x(block)
                sp.wait_ge(result_ready, DOWN_BLOCKS * KM)
                for m in range(KM):
                    sp.dma_start(tokens(d["y"][m], DOWN_BLOCKS - 1), x[:, m]).then_inc(stored, 16)
                sp.wait_ge(stored, DOWN_BLOCKS * 16 * KM)

            @block_.tensor
            def _(pe):
                def products(block, k):
                    n = block * KF + k
                    pe.wait_ge(h_ready, n + 1)
                    for m in range(KM):
                        cols = slice(m * P, m * P + P)
                        if k == 0:
                            pe.wait_ge(added, block * KM + (m + 1))
                        for j, (w, v) in enumerate(((wh, hh), (wh, hl), (wl, hh))):
                            last = pe.matmul(banks[:, m, :DOWN_W], w[:, k, cols], v[:, k % 2],
                                             start=(k == 0 and j == 0), stop=(k == KF - 1 and j == 2))
                        if k == KF - 1:
                            last.then_inc(k_done, 1)
                    if k < KF - 1:
                        last.then_inc(k_done, 1)

                pe.sem_inc(k_done, per_block)
                with pe.Fori(0, DOWN_BLOCKS) as block:
                    for k in range(KF):
                        pe.wait_ge(w_ready, k + 1)
                        products(block, k)

            @block_.scalar
            def _(act):
                with act.Fori(0, DOWN_BLOCKS) as block:
                    for k in range(KF):
                        slot, turn = h_slot(k)
                        act.wait_ge(h_loaded[slot], block * (16 * slot_turns[slot]) + 16 * (turn + 1))
                        act.wait_ge(k_done, block * per_block + (per_block + k - 1 if k >= 2 else (KF - 1, per_block)[k]))
                        nc.scalar.activation(hh[:, k % 2], h[:, slot], ACT.Copy).then_inc(h_hi, 1)
                    for m in range(KM):
                        act.wait_ge(added, block * KM + (KM + m + 1))
                        act.wait_ge(summed, block * KM + (m + 1))
                        nc.scalar.activation(square[:], x[:, m], ACT.Square).then_inc(squared, 1)
                    act.wait_ge(inverse_step, block * 2 + 2)
                    nc.scalar.activation(rstd[:], rstd[:], ACT.Sqrt).then_inc(root_ready, 1)

            @block_.gpsimd
            def _(pool):
                for block in range(DOWN_BLOCKS):
                    pool.wait_ge(summed, block * KM + (KM + 1))
                    nc.gpsimd.partition_all_reduce(rstd[:], total[:], P, bass.bass_isa.ReduceOp.add)\
                      .then_inc(total_ready, 1)

            @block_.vector
            def _(dve):
                def split_h(block, k):
                    n = block * KF + k
                    dve.wait_ge(h_hi, n + 1)
                    nc.vector.tensor_tensor(hl[:, k % 2], h[:, h_slot(k)[0]], hh[:, k % 2].bitcast(F32),
                                            ALU.subtract).then_inc(h_ready, 1)

                def finish(block, last_block):
                    dve.wait_ge(x_loaded, block * (16 * KM) + 16 * KM)
                    for m in range(KM):
                        dve.wait_ge(k_done, block * per_block + (per_block + KF + m))
                        for at, w, which in pieces(last_block):
                            last = nc.vector.scalar_tensor_tensor(
                                out=x[:, m, at:at + w], in0=banks[:, m, at:at + w],
                                scalar=mod[:, GATE2 + m, which:which + 1], in1=x[:, m, at:at + w],
                                op0=ALU.mult, op1=ALU.add)
                        last.then_inc(added, 1)
                    for m in range(KM):
                        n = block * KM + m
                        dve.wait_ge(squared, n + 1)
                        if m == 0:
                            nc.vector.tensor_copy(total[:], square[:]).then_inc(summed, 1)
                        else:
                            dve.wait_ge(summed, n + 1)
                            nc.vector.tensor_tensor(total[:], total[:], square[:], ALU.add).then_inc(summed, 1)
                    dve.wait_ge(total_ready, block + 1)
                    nc.vector.tensor_scalar(rstd[:], rstd[:], 1.0 / D_MODEL, EPS, ALU.mult, ALU.add).then_inc(inverse_step, 1)
                    dve.wait_ge(inverse_step, block * 2 + 1)
                    nc.vector.reciprocal(rstd[:], rstd[:]).then_inc(inverse_step, 1)
                    dve.wait_ge(root_ready, block + 1)
                    for m in range(KM):
                        nc.vector.scalar_tensor_tensor(out=x[:, m], in0=x[:, m], scalar=params[:, gf0 + m:gf0 + m + 1],
                                                       in1=rstd[:], op0=ALU.mult, op1=ALU.mult).then_inc(result_ready, 1)

                dve.sem_inc(added, KM)
                dve.sem_inc(summed, 1)
                for k in range(KF):
                    dve.wait_ge(w_loaded, 16 * (k + 1))
                    nc.vector.tensor_copy(wh[:, k], whole[:]).then_inc(w_hi, 1)
                    dve.wait_ge(w_hi, k + 1)
                    nc.vector.tensor_tensor(wl[:, k], whole[:], wh[:, k].bitcast(F32), ALU.subtract).then_inc(w_ready, 1)
                    split_h(0, k)
                finish(0, False)
                with dve.Fori(1, DOWN_BLOCKS - 1) as block:
                    for k in range(KF):
                        split_h(block, k)
                    finish(block, False)
                for k in range(KF):
                    split_h(DOWN_BLOCKS - 1, k)
                finish(DOWN_BLOCKS - 1, True)



def unit_root(x, n):
    return np.exp(-2j * np.pi * (x % n) / n)


def latent_tables():
    b = np.arange(64)
    first = np.zeros((2, 32, 4, 32, 2, 4))
    for half in range(2):
        a = np.arange(32) + 32 * half
        for k in range(32):
            re = unit_root(a * k, 64).real
            im = unit_root(a * k, 64).imag if k else unit_root(a * 32, 64).real
            for q in range(4):
                first[half, :, q, k, 0, q], first[half, :, q, k, 1, q] = re, im
    second = np.zeros((32, 2, 64, 2, 64))
    back1 = np.zeros((32, 2, 64, 2, 64))
    for k in range(1, 32):
        w = unit_root(b * k, 4096)[:, None] * unit_root(np.outer(b, b), 64)
        second[k, 0, :, 0], second[k, 1, :, 0], second[k, 0, :, 1], second[k, 1, :, 1] = w.real, -w.imag, w.imag, w.real
        w = w.T
        back1[k, 0, :, 0], back1[k, 1, :, 0], back1[k, 1, :, 1], back1[k, 0, :, 1] = w.real, w.imag, w.real, -w.imag
    w = unit_root(32 * b, 4096)[:, None] * unit_root(np.outer(b, np.arange(32)), 64)
    second[0, 1, :, 0, :32], second[0, 1, :, 1, :32] = w.real, w.imag
    back1[0, 0, :32, 1], back1[0, 1, :32, 1] = 2 * w.real.T, 2 * w.imag.T
    second[0, 0, :, 0, 32], second[0, 0, :, 1, 32] = 1, (-1.0) ** b
    back1[0, 0, 32, 0], back1[0, 1, 32, 0] = 1, (-1.0) ** b
    w = unit_root(np.outer(b, np.arange(1, 32)), 64)
    second[0, 0, :, 0, 33:], second[0, 0, :, 1, 33:] = w.real, w.imag
    back1[0, 0, 33:, 0], back1[0, 1, 33:, 0] = 2 * w.real.T, 2 * w.imag.T
    r = np.arange(64)
    second = second[:, :, r // 4 + 16 * (r % 4)]
    back2 = np.zeros((32, 2, 2, 32, 2))
    a = np.arange(32)
    for k in range(32):
        re = 2 * np.cos(2 * np.pi * a * k / 64) if k else np.ones(32)
        im = -2 * np.sin(2 * np.pi * a * k / 64) if k else (-1.0) ** a
        for half in range(2):
            back2[k, 0, half, :, half], back2[k, 1, half, :, half] = re / 4096, im / 4096
    return (first.reshape(2, P, 256).transpose(1, 0, 2), second.reshape(32, P, P).transpose(1, 0, 2),
            back1.reshape(32, P, P).transpose(1, 0, 2), back2.reshape(P, 64))


def context_tables():
    n, k = np.arange(256), np.arange(128)
    w = unit_root(np.outer(n, k), 256)
    re, im = w.real.copy(), w.imag.copy()
    im[:, 0] = (-1.0) ** n
    forward = np.stack([re, im], 1).reshape(2, P, 2, P)
    back_re, back_im = 2 * w.real.T[:, :P] / 256, 2 * w.imag.T[:, :P] / 256
    back_re[0] /= 2
    back_im[0] = (-1.0) ** n[:P] / 256
    return forward.transpose(1, 0, 2, 3), np.stack([back_re, back_im], 1)


def filter_tables():
    f32 = np.float32
    deltas = np.abs(np.linspace(math.log(1e-2) / 1.5, math.log(1e-2) / 0.3, D_HY, dtype=f32))
    bands = np.linspace(1e-4, HY_BANDS - 1, HY_BANDS, dtype=f32)
    feats, decay = np.zeros((P, POS), f32), np.zeros((CT, P, ROW_TILES, P), f32)
    m = np.arange(P)
    for rt in range(ROW_TILES):
        if rt < 32:
            length, n = SEQ_LAT, 2048 * (rt % 2) + 16 * m + rt // 2
        else:
            length, n = SEQ_CTX, 128 * (rt - 32) + m
        pos = np.where(n < length, n, 2 * length - n).astype(f32)
        t = pos / f32(length - 1)
        omega = f32(2.0 * math.pi) * pos / f32(length)
        angle = omega[:, None] * bands[None, :]
        feats[:1 + 2 * HY_BANDS, rt * P:rt * P + P] = np.concatenate([t[:, None], np.cos(angle), np.sin(angle)], 1).T
        row = np.exp(-t[:, None] * deltas[None, :])
        row[n == length] = 0.0
        decay[:, :, rt, :] = row.reshape(P, CT, P).transpose(1, 0, 2)
    return feats, decay



def build(nc, d):
    with ExitStack() as ctx:
        def sem(name):
            return ctx.enter_context(nc.semaphore(name))

        keep = {name: ctx.enter_context(nc.sbuf_tensor(name, shape, F32)) for name, shape in (
            ("params", [P, N_PARAMS]), ("mod", [P, N_MOD * KM, 2]), ("scale1", [P, KM, 2]), ("scale2", [P, KM, 2]),
            ("sp8", [P, 2 * CT]), ("nsp8", [P, 2 * CT]), ("ident", [P, P]), ("ones", [P, P]),
            ("zero", [P, 1]))}
        keep["norm_sems"] = norm_semaphores(sem)
        modulation(nc, sem, d, keep)
        in_proj(nc, sem, d, keep)
        rglru(nc, sem, d, keep)
        hyena(nc, sem, d, keep)
        out_proj(nc, sem, d, keep)
        ffn_up(nc, sem, d, keep)
        ffn_down(nc, sem, d, keep)


def columns(a):
    a = np.asarray(a)
    return np.ascontiguousarray(a.reshape(-1, P).T)


def pad_column(a):
    return np.concatenate([np.asarray(a), np.zeros_like(a)], -1)


def units(w, order=None):
    k, n = w.shape
    u = w.reshape(k // P, P, n // P, P).transpose(2, 1, 0, 3)
    return np.ascontiguousarray(u if order is None else u[order])


def layout(x_prompt, x_sample, state_rglru, c, c_ctx, w_ada, b_ada, g_norm1, g_norm2, w_in, rg_conv_w, rg_conv_b,
           rg_gate_w, rg_gate_b, rg_a, hy_conv_w, hy_conv_b, hf_w1, hf_b1, hf_w2, hf_b2, hf_w3, hf_freq, hy_bias,
           g_rnn_out, g_hy_out, w_out, w_up, ffn_conv_w, ffn_conv_b, w_down, g_final):
    f32 = np.float32
    order_in = list(range(CT)) + list(range(2 * CT, 5 * CT)) + list(range(CT, 2 * CT))
    conv_w = np.concatenate([rg_conv_w[0], np.concatenate([np.zeros((1, 3 * D_HY), f32), hy_conv_w[0]], 0)], 1)
    parts = {
        "g1": columns(g_norm1[0]), "g2": columns(g_norm2[0]), "gf": columns(g_final),
        "go": np.concatenate([columns(g_rnn_out[0]), columns(g_hy_out[0])], 1),
        "cw": np.ascontiguousarray(conv_w.reshape(4, N_CONV, P).transpose(2, 1, 0)).reshape(P, 4 * N_CONV),
        "cb": np.concatenate([columns(rg_conv_b[0]), columns(hy_conv_b[0])], 1),
        "gate_b": columns(rg_gate_b[0]), "rg_a": columns(rg_a[0]), "h0": columns(state_rglru[0, 0]),
        "hy_b": columns(hy_bias[0]), "ffn_w": columns(ffn_conv_w[0]), "ffn_b": columns(ffn_conv_b[0]),
        "mlp_b": columns(np.concatenate([pad_column(hf_b1[0]), pad_column(hf_b2[0])])),
        "mlp_f": columns(pad_column(hf_freq[0])),
    }
    first, second, back1, back2 = latent_tables()
    ctx_forward, ctx_back = context_tables()
    feats, decay = filter_tables()
    up = units(w_up[0])
    arrays = {
        "xT": np.concatenate([x_sample[0], x_prompt[0]], 0).T.reshape(KM, P, T),
        "cond": np.stack([c[0].reshape(KM, P), c_ctx.reshape(KM, P)], -1).transpose(1, 0, 2),
        "params": np.concatenate([parts[name] for name in PARAMS], 1),
        "ada_bias": np.stack([b_ada[0], b_ada[0]]),
        "w_ada": w_ada[0].reshape(KM, P, 12, 512).transpose(2, 1, 0, 3),
        "w_in": units(w_in[0], order_in),
        "gate_w": rg_gate_w[0].reshape(4, CT, 2, 64, 64).transpose(2, 3, 0, 1, 4).reshape(2, 64, 4 * CT, 64),
        "mlp_w1": hf_w1[0], "mlp_w2": hf_w2[0],
        "mlp_w3": hf_w3[0].reshape(64, 2, 2, CT, P).transpose(1, 3, 0, 2, 4),
        "w_out": units(w_out[0]),
        "w_up": np.stack([up[KF:], up[:KF]], 1).reshape(2 * KF, P, KM, P),
        "w_down": w_down[0].reshape(KF, P, D_MODEL),
        "ident": np.eye(P, dtype=f32), "feats": feats, "decay": decay,
        "first_table": first.astype(f32), "second_table": second.astype(f32), "back1_table": back1.astype(f32),
        "back2_table": back2.astype(f32), "ctx_forward_table": ctx_forward.astype(f32),
        "ctx_back_table": ctx_back.astype(f32),
    }
    return {name: np.ascontiguousarray(a) for name, a in arrays.items()}


SCRATCH = {"pre": [N_IN, P, T], "mixed": [KM, P, T], "x1": [KM, P, T], "hidden_ff": [KF, P, T], "hidden": [P, POS]}
OUTPUTS = {"y": [KM, P, T], "states": [P, CT, 2]}


def kernel(**inputs):
    import concourse.bacc as bacc
    from concourse.bass_utils import run_bass_kernel_spmd

    nc = bacc.Bacc("TRN2", target_bir_lowering=False, num_devices=1)
    arrays = layout(**{name: np.asarray(a) for name, a in inputs.items()})
    d = {name: nc.dram_tensor(name + "_in", list(a.shape), F32, kind="ExternalInput").ap() for name, a in arrays.items()}
    d.update({name: nc.dram_tensor(name + "_dram", shape, F32, kind="Internal").ap() for name, shape in SCRATCH.items()})
    d.update({name: nc.dram_tensor(name + "_out", shape, F32, kind="ExternalOutput").ap()
              for name, shape in OUTPUTS.items()})
    build(nc, d)
    r = run_bass_kernel_spmd(nc, [{name + "_in": a for name, a in arrays.items()}], core_ids=[0])
    y = r.results[0]["y_out"].reshape(D_MODEL, T).T
    states = r.results[0]["states_out"].transpose(2, 1, 0).reshape(1, 1, 2, D_RNN)
    return (np.ascontiguousarray(y[SEQ_LAT:])[None], np.ascontiguousarray(y[:SEQ_LAT])[None],
            np.ascontiguousarray(states))
```

```python
import math
from contextlib import ExitStack

import numpy as np

import concourse.bass as bass
from concourse import mybir
from concourse.alu_op_type import AluOpType as ALU

F32 = mybir.dt.float32
F32R = mybir.dt.float32r
ACT = mybir.ActivationFunctionType

P = 128
D_MODEL = 1024
KM = D_MODEL // P
SEQ_LAT, SEQ_CTX = 2048, 128
T = SEQ_LAT + SEQ_CTX
GRID_W = 64
GRID_H = SEQ_LAT // GRID_W
D_RNN = D_HY = 512
CT = D_RNN // P
D_FF = 2816
KF = D_FF // P
HY_BANDS = 16
N_MOD = 6
EPS = 1e-6
RG_C = 8.0
N_CONV = 4 * CT
N_IN = 5 * CT
TOKEN_BLOCKS = [(0, 448), (448, 448), (896, 448), (1344, 448), (1792, 384)]
NB = len(TOKEN_BLOCKS)
CTX_AT = SEQ_LAT
POS_LAT, POS_CTX = 2 * SEQ_LAT, 2 * SEQ_CTX
POS = POS_LAT + POS_CTX
POS_BLOCKS = [(s, min(512, POS - s)) for s in range(0, POS, 512)]
ROW_TILES = POS // P
PARAMS = {}
for _name, _width in (("g1", KM), ("g2", KM), ("go", KM), ("gf", KM), ("cw", 4 * N_CONV), ("cb", N_CONV),
                      ("gate_b", 4 * CT), ("rg_a", 2 * CT), ("h0", 2 * CT), ("hy_b", 2 * CT),
                      ("ffn_w", 9 * KF), ("ffn_b", KF), ("mlp_b", 2), ("mlp_f", 2)):
    PARAMS[_name] = (sum(w for _, w in PARAMS.values()), _width)
N_PARAMS = sum(w for _, w in PARAMS.values())
SHIFT1, SCALE1, GATE1, SHIFT2, SCALE2, GATE2 = (KM * j for j in range(N_MOD))
LAT, CTX = 0, 1
PAD_AT_LAT, PAD_AT_CTX = 2, 2 + SEQ_LAT + 3
PAD_LEN = PAD_AT_CTX + SEQ_CTX + 1


class Steps:

    def __init__(self, engine, sem, start=0):
        self.engine, self.sem, self.start, self.n = engine, sem, start, 0

    def done(self, instruction):
        self.n += 1
        instruction.then_inc(self.sem, 1)

    def wait(self):
        self.engine.wait_ge(self.sem, self.start + self.n)


def segments(start, width):
    cut = min(max(CTX_AT, start), start + width)
    return [(s, w, m) for s, w, m in ((start, cut - start, LAT), (cut, start + width - cut, CTX)) if w]



NORM_BLOCKS = [(s, min(256, T - s)) for s in range(0, T, 256)]
NNB = len(NORM_BLOCKS)
SCALED_SLOTS = 4


def norm_semaphores(sem):
    names = ["x_loaded0", "x_loaded1", "x_loaded2", "squared", "folded", "summed", "mean_ready", "inverse_ready", "root_ready",
             "rstd_ready", "scaled_ready", "hi_ready", "lo_ready"]
    return {name: sem("norm_" + name) for name in names}, {name: 0 for name in names}


def norm_buffers(sb, norm_sems, tag, groups, sum_bank, rstd_banks, lent):
    sems, starts = norm_sems
    at_start = dict(starts)
    x = sb(tag + "_norm_x", [P, 2, KM, 256], F32)
    for name in starts:
        starts[name] += (16 * len(NORM_BLOCKS[int(name[-1])::3]) if name.startswith("x_loaded")
                         else NNB * (3 if groups == 1 else 2) if name == "folded"
                         else NNB if name in ("summed", "mean_ready", "inverse_ready", "root_ready", "rstd_ready") else KM * NNB)
    return {
        "groups": groups,
        "x": [x[:, 0], x[:, 1], lent[:, :KM * 256].rearrange("p (k t) -> p k t", k=KM)],
        "square": sb(tag + "_norm_square", [P, KM, 256], F32),
        "columns": sb(tag + "_norm_columns", [P, 2 * groups], F32),
        "scaled": sb(tag + "_norm_scaled", [P, SCALED_SLOTS, 256], F32),
        "sums": sum_bank[:, 0:2 * groups],
        "rstd": [bank.rearrange("p (g t) -> p g t", g=2) for bank in rstd_banks],
        "sems": sems,
        "start": at_start,
    }


def norm_wait(engine, nb, name, count):
    engine.wait_ge(nb["sems"][name], nb["start"][name] + count)


def norm_inc(instruction, nb, name):
    instruction.then_inc(nb["sems"][name], 1)


def norm_load(sp, nb, source, b):
    s, w = NORM_BLOCKS[b]
    if b >= 3:
        norm_wait(sp, nb, "scaled_ready", KM * (b - 2))
    sp.dma_start(nb["x"][b % 3][:, :, :w], source.rearrange("k p t -> p k t")[:, :, s:s + w])\
      .then_inc(nb["sems"][f"x_loaded{b % 3}"], 16)


def norm_scalar(nc, act, nb, shift, xh):
    def square(b, k):
        if k == 0:
            norm_wait(act, nb, f"x_loaded{b % 3}", 16 * (b // 3 + 1))
            if b:
                norm_wait(act, nb, "summed", b)
        w = NORM_BLOCKS[b][1]
        norm_inc(nc.scalar.activation(nb["square"][:, k, :w], nb["x"][b % 3][:, k, :w], ACT.Square), nb, "squared")

    def root(b):
        norm_wait(act, nb, "inverse_ready", b + 1)
        norm_inc(nc.scalar.activation(nb["columns"][:], nb["columns"][:], ACT.Sqrt), nb, "root_ready")

    def high(b, k):
        s, w = NORM_BLOCKS[b]
        m = LAT if s < CTX_AT else CTX
        n = KM * b + k
        norm_wait(act, nb, "scaled_ready", n + 1)
        scaled = nb["scaled"][:, n % SCALED_SLOTS, :w]
        if shift is None:
            hi = nc.scalar.activation(xh[:, k, s:s + w], scaled, ACT.Copy)
        else:
            hi = nc.scalar.activation(xh[:, k, s:s + w], scaled, ACT.Identity, bias=shift[:, k, m:m + 1])
        norm_inc(hi, nb, "hi_ready")

    for k in range(KM):
        square(0, k)
    root(0)
    for k in range(KM):
        square(1, k)
    for b in range(NNB):
        for k in range(KM):
            if b + 2 < NNB and k >= KM // 2:
                square(b + 2, 2 * k - KM)
                square(b + 2, 2 * k - KM + 1)
            high(b, k)
            if b + 1 < NNB and k == 5:
                root(b + 1)


def norm_vector(nc, dve, nb, scale, shift, xh, xl):
    groups = nb["groups"]

    def inverse(b):
        norm_wait(dve, nb, "summed", b + 1)
        if b:
            norm_wait(dve, nb, "rstd_ready", b)
        norm_inc(nc.vector.tensor_scalar(nb["columns"][:], nb["sums"], 1.0 * groups / D_MODEL, EPS,
                                         ALU.mult, ALU.add), nb, "mean_ready")
        norm_wait(dve, nb, "mean_ready", b + 1)
        norm_inc(nc.vector.reciprocal(nb["columns"][:], nb["columns"][:]), nb, "inverse_ready")

    def scaled(b, k):
        s, w = NORM_BLOCKS[b]
        m = LAT if s < CTX_AT else CTX
        n = KM * b + k
        if k == 0:
            norm_wait(dve, nb, "rstd_ready", b + 1)
        if n >= SCALED_SLOTS:
            norm_wait(dve, nb, "lo_ready", n - SCALED_SLOTS + 1)
        norm_inc(nc.vector.scalar_tensor_tensor(
            out=nb["scaled"][:, n % SCALED_SLOTS, :w], in0=nb["x"][b % 3][:, k, :w], scalar=scale[:, k, m:m + 1],
            in1=nb["rstd"][b % 2][:, k * groups // KM, :w], op0=ALU.mult, op1=ALU.mult), nb, "scaled_ready")

    def low(b, k):
        s, w = NORM_BLOCKS[b]
        m = LAT if s < CTX_AT else CTX
        n = KM * b + k
        norm_wait(dve, nb, "hi_ready", n + 1)
        value, hi = nb["scaled"][:, n % SCALED_SLOTS, :w], xh[:, k, s:s + w].bitcast(F32)
        if shift is None:
            lo = nc.vector.tensor_tensor(xl[:, k, s:s + w], value, hi, ALU.subtract)
        else:
            lo = nc.vector.scalar_tensor_tensor(out=xl[:, k, s:s + w], in0=value, scalar=shift[:, k, m:m + 1],
                                                in1=hi, op0=ALU.add, op1=ALU.subtract)
        norm_inc(lo, nb, "lo_ready")

    inverse(0)
    lag = SCALED_SLOTS - 2
    for n in range(KM * NNB + lag):
        if n < KM * NNB:
            scaled(n // KM, n % KM)
        if n >= lag:
            low((n - lag) // KM, (n - lag) % KM)
        if n % KM == 6 and n // KM + 1 < NNB:
            inverse(n // KM + 1)


def norm_gpsimd(nc, pool, nb, b):
    groups, levels = nb["groups"], 3 if nb["groups"] == 1 else 2
    w = NORM_BLOCKS[b][1]
    norm_wait(pool, nb, "squared", KM * (b + 1))
    for level in range(levels):
        half = KM // groups >> (level + 1)
        if level:
            norm_wait(pool, nb, "folded", levels * b + level)
        for g in range(groups):
            at = g * KM // groups
            last = nc.gpsimd.tensor_tensor(nb["square"][:, at:at + half, :w], nb["square"][:, at:at + half, :w],
                                           nb["square"][:, at + half:at + 2 * half, :w], ALU.add)
        norm_inc(last, nb, "folded")


def norm_tensor(pe, nb, ones, ident, first_product):
    groups = nb["groups"]

    def sums(b):
        if b:
            norm_wait(pe, nb, "mean_ready", b)
        norm_wait(pe, nb, "folded", (3 if groups == 1 else 2) * (b + 1))
        for g in range(groups):
            for tile in range(NORM_BLOCKS[b][1] // P):
                mm = pe.matmul(nb["sums"][:, 2 * g + tile:2 * g + tile + 1],
                               nb["square"][:, g * KM // groups, tile * P:tile * P + P], ones[:, 0:1],
                               start=True, stop=True)
        norm_inc(mm, nb, "summed")

    def spread(b):
        norm_wait(pe, nb, "root_ready", b + 1)
        if b >= 2:
            norm_wait(pe, nb, "scaled_ready", KM * (b - 1))
        for g in range(groups):
            for tile in range(NORM_BLOCKS[b][1] // P):
                at = 2 * g + tile
                mm = pe.matmul(nb["rstd"][b % 2][:, g, tile * P:tile * P + P],
                               nb["columns"][:, at:at + 1].broadcast_to([P, P]), ident[:], start=True, stop=True)
        norm_inc(mm, nb, "rstd_ready")

    sums(0)
    spread(0)
    sums(1)
    done = 0
    for b in range(NNB):
        if b + 1 < NNB:
            spread(b + 1)
        if sum(TOKEN_BLOCKS[done]) <= 256 * b:
            first_product(done)
            done += 1
        if b + 2 < NNB:
            sums(b + 2)
    for i in range(done, NB):
        first_product(i)


def wait_for_block(pe, nb, i):
    norm_wait(pe, nb, "lo_ready", KM * -(-sum(TOKEN_BLOCKS[i]) // 256))



def weight_buffers(sb, sem, zero, tag):
    return {
        "zero": zero[:].unsqueeze(2).broadcast_to([P, KM, P]),
        "whole": sb(tag + "_w_whole", [P, KM, P], F32),
        "hi": sb(tag + "_w_hi", [P, 2, KM, P], F32R),
        "lo": sb(tag + "_w_lo", [P, 2, KM, P], F32R),
        "loaded": sem(f"{tag}_w_loaded"),
        "hi_ready": sem(f"{tag}_w_hi_ready"),
        "ready": sem(f"{tag}_w_ready"),
        "block_done": sem(f"{tag}_block_done"),
    }


def weight_split(nc, pool, wb, n, u, first=False):
    pool.wait_ge(wb["loaded"], n * 16 + 16)
    if not first:
        pool.wait_ge(wb["block_done"], (n - 1) * NB)
    nc.gpsimd.tensor_tensor(wb["hi"][:, u], wb["whole"][:], wb["zero"], ALU.add).then_inc(wb["hi_ready"], 1)
    pool.wait_ge(wb["hi_ready"], n + 1)
    nc.gpsimd.tensor_tensor(wb["lo"][:, u], wb["whole"][:], wb["hi"][:, u].bitcast(F32),
                            ALU.subtract).then_inc(wb["ready"], 1)


def norm_and_weight_splits(nc, pool, nb, wb, units):
    for b in range(NNB):
        norm_gpsimd(nc, pool, nb, b)
        if b in (0, 3):
            weight_split(nc, pool, wb, b // 3, b // 3, first=True)
    with pool.Fori(1, units // 2) as pair:
        for u in range(2):
            weight_split(nc, pool, wb, pair * 2 + u, u)


def product_block(pe, out, wb, u, xh, xl, s, w):
    parts = [(wb["hi"], xh), (wb["hi"], xl), (wb["lo"], xh)]
    for k in range(KM):
        for j, (weight, x) in enumerate(parts):
            last = pe.matmul(out, weight[:, u, k], x[:, k, s:s + w],
                             start=(k == 0 and j == 0), stop=(k == KM - 1 and j == 2))
    last.then_inc(wb["block_done"], 1)



def modulation(nc, sem, d, keep):
    chunks, width = N_MOD * D_MODEL // 512, 512
    two_pi_hi = 6.28125
    two_pi_lo = 2 * math.pi - two_pi_hi
    round_magic = 1.5 * 2.0 ** 23
    pi_below = 3.1415925
    npos = len(POS_BLOCKS)
    sine_steps = 5
    with ExitStack() as ctx:
        def sb(name, shape, dt=F32):
            return ctx.enter_context(nc.sbuf_tensor(name, shape, dt))

        cond, act_c = sb("cond", [P, KM, 2]), sb("act_c", [P, KM, 2])
        wada = sb("wada", [P, 3, KM, width])
        bias = sb("ada_bias", [2, N_MOD * D_MODEL])
        rows = sb("mod_rows", [2, N_MOD * D_MODEL])
        work = sb("softplus_work", [P, 6, 2 * CT])
        feats = sb("feats", [P, POS])
        hidden = sb("hidden", [P, POS])
        w1, w2 = sb("mlp_w1", [P, P]), sb("mlp_w2", [P, P])
        bf = sb("mlp_bf", [P, 2])
        angle, turns = sb("angle", [P, 2, 512]), sb("turns", [P, 2, 512])
        ps = ctx.enter_context(nc.psum_tensor("mod_psum", [2, 2, 512], F32))
        turned = ctx.enter_context(nc.psum_tensor("mod_turned", [P, N_MOD * KM, 2], F32))
        ps_mlp = ctx.enter_context(nc.psum_tensor("mlp_psum", [P, 4, 512], F32))
        params, mod, scale1, scale2, sp8, nsp8, ident, ones = (keep[x] for x in (
            "params", "mod", "scale1", "scale2", "sp8", "nsp8", "ident", "ones"))
        loaded = sem("mod_loaded")
        w_loaded = [sem(f"ada_loaded{u}") for u in range(3)]
        silu_done, exp_done = sem("silu_done"), sem("exp_a_done")
        chunk_done, row_done, turn_done = sem("ada_chunk_done"), sem("ada_row_done"), sem("mod_turn_done")
        ones_done, dve_step = sem("ones_done"), sem("mod_dve_step")
        mlp_zeroed, mlp_loaded, feats_loaded = sem("mlp_zeroed"), sem("mlp_loaded"), sem("feats_loaded")
        mlp_mm, angle_ready, angle_step, turns_done, sine_done, hidden_stored = (sem(x) for x in (
            "mlp_mm", "angle_ready", "angle_step", "turns_done", "sine_done", "hidden_stored"))

        mlp_order = []
        for c in range(chunks):
            mlp_order.append([(0, c)] * (c < npos) + [(1, c - 3)] * (3 <= c < npos + 3))
        flat = [x for step in mlp_order for x in step]

        with nc.Block() as block:
            @block.sync
            def _(sp):
                for dst, src in ((cond, d["cond"]), (params, d["params"]), (bias, d["ada_bias"]), (ident, d["ident"])):
                    sp.dma_start(dst[:], src).then_inc(loaded, 16)
                sp.wait_ge(mlp_zeroed, 2)
                sp.dma_start(w1[0:1 + 2 * HY_BANDS, 0:64], d["mlp_w1"]).then_inc(mlp_loaded, 16)
                sp.dma_start(w2[0:64, 0:64], d["mlp_w2"]).then_inc(mlp_loaded, 16)
                sp.dma_start(feats[:], d["feats"]).then_inc(feats_loaded, 16)
                for c in range(chunks):
                    if c >= 3:
                        sp.wait_ge(chunk_done, c - 2)
                    sp.dma_start(wada[:, c % 3], d["w_ada"][c]).then_inc(w_loaded[c % 3], 16)
                sp.wait_ge(sine_done, 2 * npos)
                sp.dma_start(d["hidden"], hidden[:]).then_inc(hidden_stored, 16)
                sp.wait_ge(hidden_stored, 16)

            @block.scalar
            def _(act):
                act.wait_ge(loaded, 64)
                nc.scalar.activation(act_c[:], cond[:], ACT.Silu).then_inc(silu_done, 1)
                act.wait_ge(dve_step, 1)
                nc.scalar.activation(work[:, 1, :], work[:, 0, :], ACT.Exp).then_inc(exp_done, 1)
                for n, (layer, b) in enumerate(flat):
                    s, w = POS_BLOCKS[b]
                    act.wait_ge(angle_ready, n + 1)
                    out = feats if layer == 0 else hidden
                    nc.scalar.activation(out[:, s:s + w], angle[:, n % 2, :w], ACT.Sin).then_inc(sine_done, 1)

            @block.vector
            def _(dve):
                own = Steps(dve, dve_step)
                a0, a1 = PARAMS["rg_a"]
                a = params[:, a0:a0 + a1]
                dve.wait_ge(loaded, 64)
                own.done(nc.vector.scalar_tensor_tensor(out=work[:, 0, :], in0=a, scalar=-1.0, in1=a,
                                                        op0=ALU.mult, op1=ALU.min))
                dve.wait_ge(exp_done, 1)
                own.done(nc.vector.tensor_scalar(work[:, 2, :], work[:, 1, :], 2.0, None, ALU.add))
                own.wait()
                own.done(nc.vector.reciprocal(work[:, 3, :], work[:, 2, :]))
                own.wait()
                own.done(nc.vector.tensor_tensor(work[:, 2, :], work[:, 1, :], work[:, 3, :], ALU.mult))
                own.wait()
                own.done(nc.vector.tensor_tensor(work[:, 3, :], work[:, 2, :], work[:, 2, :], ALU.mult))
                own.done(nc.vector.memset(work[:, 4, :], 1.0 / 19))
                own.wait()
                for odd in range(17, 0, -2):
                    own.done(nc.vector.tensor_tensor(work[:, 4, :], work[:, 4, :], work[:, 3, :], ALU.mult))
                    own.wait()
                    own.done(nc.vector.tensor_scalar(work[:, 4, :], work[:, 4, :], 1.0 / odd, None, ALU.add))
                    own.wait()
                own.done(nc.vector.scalar_tensor_tensor(out=work[:, 4, :], in0=work[:, 4, :], scalar=2.0,
                                                        in1=work[:, 2, :], op0=ALU.mult, op1=ALU.mult))
                own.done(nc.vector.tensor_scalar(work[:, 5, :], a, -1.0, 0.0, ALU.mult, ALU.max))
                own.wait()
                own.done(nc.vector.tensor_tensor(work[:, 5, :], work[:, 5, :], work[:, 4, :], ALU.add))
                own.wait()
                own.done(nc.vector.tensor_scalar(sp8[:], work[:, 5, :], RG_C, None, ALU.mult))
                own.done(nc.vector.tensor_scalar(nsp8[:], work[:, 5, :], -RG_C, None, ALU.mult))
                b0, f0 = PARAMS["mlp_b"][0], PARAMS["mlp_f"][0]
                own.done(nc.vector.tensor_tensor(bf[:], params[:, b0:b0 + 2], params[:, f0:f0 + 2], ALU.mult))
                own.wait()

                def reduce_angle(n, layer, b):
                    s, w = POS_BLOCKS[b]
                    x, k = angle[:, n % 2, :w], turns[:, n % 2, :w]
                    step = Steps(dve, angle_step, n * (sine_steps - 1))
                    dve.wait_ge(mlp_mm, n + 1)
                    if n >= 2:
                        dve.wait_ge(sine_done, n - 1)
                    step.done(nc.vector.tensor_scalar(x, ps_mlp[:, n % 4, :w], params[:, f0 + layer:f0 + layer + 1],
                                                      bf[:, layer:layer + 1], ALU.mult, ALU.add))
                    step.wait()
                    step.done(nc.vector.tensor_scalar(k, x, 1 / (2 * math.pi), round_magic, ALU.mult, ALU.add))
                    step.wait()
                    step.done(nc.vector.tensor_scalar(k, k, -round_magic, None, ALU.add))
                    step.wait()
                    step.done(nc.vector.scalar_tensor_tensor(out=x, in0=k, scalar=-two_pi_hi, in1=x,
                                                             op0=ALU.mult, op1=ALU.add))
                    step.wait()
                    assert step.n == sine_steps - 1
                    nc.vector.scalar_tensor_tensor(out=x, in0=k, scalar=-two_pi_lo, in1=x,
                                                   op0=ALU.mult, op1=ALU.add).then_inc(turns_done, 1)
                    dve.wait_ge(turns_done, n + 1)
                    nc.vector.tensor_scalar(x, x, pi_below, -pi_below, ALU.min, ALU.max).then_inc(angle_ready, 1)

                n = 0
                for c in range(chunks):
                    dve.wait_ge(chunk_done, c + 1)
                    at = c * width
                    nc.vector.tensor_tensor(rows[:, at:at + width], ps[:, c % 2, :], bias[:, at:at + width],
                                            ALU.add).then_inc(row_done, 1)
                    for layer, b in mlp_order[c]:
                        reduce_angle(n, layer, b)
                        n += 1
                dve.wait_ge(turn_done, 1)
                own.done(nc.vector.tensor_copy(mod[:], turned[:]))
                own.wait()
                for scale, at, g in ((scale1, SCALE1, "g1"), (scale2, SCALE2, "g2")):
                    g0, gw = PARAMS[g]
                    gain = params[:, g0:g0 + gw].unsqueeze(2).broadcast_to([P, KM, 2])
                    own.done(nc.vector.scalar_tensor_tensor(out=scale[:], in0=mod[:, at:at + KM, :], scalar=1.0,
                                                            in1=gain, op0=ALU.add, op1=ALU.mult))

            @block.gpsimd
            def _(pool):
                nc.gpsimd.memset(w1[:], 0.0).then_inc(mlp_zeroed, 1)
                nc.gpsimd.memset(w2[:], 0.0).then_inc(mlp_zeroed, 1)
                nc.gpsimd.memset(ones[:], 1.0).then_inc(ones_done, 1)
                nc.gpsimd.memset(keep["zero"][:], 0.0).then_inc(ones_done, 1)
                pool.wait_ge(ones_done, 2)

            @block.tensor
            def _(pe):
                pe.wait_ge(silu_done, 1)
                n = 0
                for c in range(chunks):
                    for layer, b in mlp_order[c]:
                        s, w = POS_BLOCKS[b]
                        if n == 0:
                            pe.wait_ge(mlp_loaded, 32)
                            pe.wait_ge(feats_loaded, 16)
                        if layer == 1:
                            pe.wait_ge(sine_done, flat.index((0, b)) + 1)
                        if n >= 4:
                            pe.wait_ge(angle_step, (n - 4) * (sine_steps - 1) + 1)
                        pe.matmul(ps_mlp[:, n % 4, :w], (w2 if layer else w1)[:], feats[:, s:s + w],
                                  start=True, stop=True).then_inc(mlp_mm, 1)
                        n += 1
                    pe.wait_ge(w_loaded[c % 3], c // 3 * 16 + 16)
                    if c >= 2:
                        pe.wait_ge(row_done, c - 1)
                    for k in range(KM):
                        last = pe.matmul(ps[:, c % 2, :], act_c[:, k, :], wada[:, c % 3, k, :],
                                         start=(k == 0), stop=(k == KM - 1))
                    last.then_inc(chunk_done, 1)
                pe.wait_ge(row_done, chunks)
                for j in range(N_MOD * KM):
                    last = pe.transpose(turned[:, j, :], rows[:, j * P:(j + 1) * P], ident[0:2, 0:2])
                last.then_inc(turn_done, 1)


def in_proj(nc, sem, d, keep):
    with ExitStack() as ctx:
        def sb(name, shape, dt=F32):
            return ctx.enter_context(nc.sbuf_tensor(name, shape, dt))

        def psum(name, shape, dt=F32):
            return ctx.enter_context(nc.psum_tensor(name, shape, dt))

        xh, xl = sb("xh", [P, KM, T], F32R), sb("xl", [P, KM, T], F32R)
        padded = sb("padded", [P, PAD_LEN])
        norm_banks, banks = psum("in_norm_banks", [P, 3, 512]), psum("in_banks", [P, NB, 512])
        nb = norm_buffers(sb, keep["norm_sems"], "in", 1, norm_banks[:, 0], [norm_banks[:, 1], norm_banks[:, 2]],
                          padded)
        wb = weight_buffers(sb, sem, keep["zero"], "in")
        result = sb("in_result", [P, T])
        bank_free, pads_zero, tap_done, result_ready, result_stored = (sem(x) for x in (
            "in_bank_free", "in_pads_zero", "in_tap_done", "in_result_ready", "in_result_stored"))
        params, ones = keep["params"], keep["ones"]
        shift = keep["mod"][:, SHIFT1:SHIFT1 + KM, :]
        cw0, cb0 = PARAMS["cw"][0], PARAMS["cb"][0]

        with nc.Block() as block:
            @block.sync
            def _(sp):
                norm_load(sp, nb, d["xT"], 0)
                sp.dma_start(wb["whole"][:], d["w_in"][0]).then_inc(wb["loaded"], 16)
                norm_load(sp, nb, d["xT"], 1)
                sp.wait_ge(wb["ready"], 1)
                sp.dma_start(wb["whole"][:], d["w_in"][1]).then_inc(wb["loaded"], 16)
                for b in range(2, NNB):
                    norm_load(sp, nb, d["xT"], b)
                with sp.Fori(2, N_IN) as n:
                    sp.wait_ge(wb["ready"], n)
                    sp.dma_start(wb["whole"][:], d["w_in"][n]).then_inc(wb["loaded"], 16)
                    sp.wait_ge(result_ready, n - 1)
                    sp.dma_start(d["pre"][n - 2], result[:]).then_inc(result_stored, 16)
                for n in range(N_IN - 2, N_IN):
                    sp.wait_ge(result_ready, n + 1)
                    sp.dma_start(d["pre"][n], result[:]).then_inc(result_stored, 16)
                sp.wait_ge(result_stored, 16 * (N_IN + 1))

            @block.scalar
            def _(act):
                norm_scalar(nc, act, nb, shift, xh)
                act.wait_ge(pads_zero, 1)
                with act.Fori(0, N_CONV) as n:
                    for b, (s, w) in enumerate(TOKEN_BLOCKS):
                        act.wait_ge(wb["block_done"], n * NB + b + 1)
                        for at, width, m in segments(s, w):
                            to = at + (PAD_AT_LAT if m == LAT else PAD_AT_CTX - CTX_AT)
                            last = nc.scalar.activation(padded[:, to:to + width], banks[:, b, at - s:at - s + width],
                                                        ACT.Copy)
                        last.then_inc(bank_free, 1)
                    act.wait_ge(result_ready, n + 1)
                with act.Fori(N_CONV, N_IN) as n:
                    act.wait_ge(result_stored, n * 16 + 16)
                    for b, (s, w) in enumerate(TOKEN_BLOCKS):
                        act.wait_ge(wb["block_done"], n * NB + b + 1)
                        nc.scalar.activation(result[:, s:s + w], banks[:, b, :w],
                                             ACT.Gelu_apprx_tanh).then_inc(bank_free, 1)
                    act.wait_ge(bank_free, n * NB + NB)
                    act.sem_inc(result_ready, 1)

            @block.vector
            def _(dve):
                norm_vector(nc, dve, nb, keep["scale1"], shift, xh, xl)
                nc.vector.memset(padded[:], 0.0).then_inc(pads_zero, 1)
                dve.sem_inc(result_stored, 16)
                with dve.Fori(0, N_CONV) as n:
                    own = Steps(dve, tap_done, n * 3)
                    dve.wait_ge(bank_free, n * NB + NB)
                    dve.wait_ge(result_stored, n * 16 + 16)
                    for tap in range(4):
                        weight = params[:, bass.ds(n * 4 + (cw0 + tap), 1)]
                        for to, at, width in ((0, 0, SEQ_LAT), (CTX_AT, PAD_AT_CTX - PAD_AT_LAT, SEQ_CTX)):
                            x, y = padded[:, at + tap:at + tap + width], result[:, to:to + width]
                            if tap == 0:
                                last = nc.vector.tensor_scalar(y, x, weight, params[:, bass.ds(n + cb0, 1)],
                                                               ALU.mult, ALU.add)
                            else:
                                last = nc.vector.scalar_tensor_tensor(out=y, in0=x, scalar=weight, in1=y,
                                                                      op0=ALU.mult, op1=ALU.add)
                        if tap < 3:
                            own.done(last)
                            own.wait()
                        else:
                            last.then_inc(result_ready, 1)

            @block.gpsimd
            def _(pool):
                norm_and_weight_splits(nc, pool, nb, wb, N_IN)

            @block.tensor
            def _(pe):
                def first_product(b):
                    s, w = TOKEN_BLOCKS[b]
                    if b == 0:
                        pe.wait_ge(wb["ready"], 1)
                    wait_for_block(pe, nb, b)
                    product_block(pe, banks[:, b, :w], wb, 0, xh, xl, s, w)

                def unit(n, u):
                    pe.wait_ge(wb["ready"], n + 1)
                    for b, (s, w) in enumerate(TOKEN_BLOCKS):
                        pe.wait_ge(bank_free, (n - 1) * NB + b + 1)
                        product_block(pe, banks[:, b, :w], wb, u, xh, xl, s, w)

                norm_tensor(pe, nb, ones, keep["ident"], first_product)
                unit(1, 1)
                with pe.Fori(1, N_IN // 2) as pair:
                    for u in range(2):
                        unit(pair * 2 + u, u)


def rglru(nc, sem, d, keep):
    with ExitStack() as ctx:
        def sb(name, shape, dt=F32):
            return ctx.enter_context(nc.sbuf_tensor(name, shape, dt))

        gate_w = sb("gate_w", [P, 4 * CT, P])
        x, gy = sb("rg_x", [P, 2, T]), sb("rg_gelu_y", [P, 2, T])
        r, i, a, s2 = (sb(name, [P, 2, 2, T]) for name in ("rg_r", "rg_i", "rg_a", "rg_s"))
        states = sb("rg_states", [P, CT, 2])
        banks = ctx.enter_context(nc.psum_tensor("rg_banks", [P, 8, 512], F32))
        zeroed, w_loaded, gate_mm, gate_done = (sem(q) for q in ("rg_zeroed", "rg_w_loaded", "rg_gate_mm", "rg_gate_done"))
        x_loaded, y_loaded = [sem("rg_x_loaded0"), sem("rg_x_loaded1")], [sem("rg_y_loaded0"), sem("rg_y_loaded1")]
        decay_done, squared, one_minus, root_done, gated, input_ready, scanned, summed, out_ready, state_done = (
            sem("rg_" + q) for q in ("decay_done", "squared", "one_minus", "root_done", "gated", "input_ready",
                                     "scanned", "summed", "out_ready", "state_done"))
        stored = [sem("rg_stored0"), sem("rg_stored1")]
        params = keep["params"]
        gb0, h00 = PARAMS["gate_b"][0], PARAMS["h0"][0]

        with nc.Block() as block:
            @block.sync
            def _(sp):
                sp.dma_start(x[:, 0], d["pre"][0]).then_inc(x_loaded[0], 16)
                sp.wait_ge(zeroed, 1)
                for half in range(2):
                    q = slice(64 * half, 64 * half + 64)
                    sp.dma_start(gate_w[q, :, q], d["gate_w"][half]).then_inc(w_loaded, 16)
                for ct in range(CT):
                    if ct >= 2:
                        sp.wait_ge(gated, 2 * (ct - 1))
                    if ct:
                        sp.dma_start(x[:, ct % 2], d["pre"][ct]).then_inc(x_loaded[ct % 2], 16)
                    if ct >= 2:
                        sp.wait_ge(out_ready, ct - 1)
                        sp.dma_start(d["mixed"][ct - 2], s2[:, ct % 2, 0]).then_inc(stored[ct % 2], 16)
                    sp.dma_start(gy[:, ct % 2], d["pre"][N_CONV + ct]).then_inc(y_loaded[ct % 2], 16)
                for ct in (CT - 2, CT - 1):
                    sp.wait_ge(out_ready, ct + 1)
                    sp.dma_start(d["mixed"][ct], s2[:, ct % 2, 0]).then_inc(stored[ct % 2], 16)
                sp.wait_ge(state_done, 2 * CT)
                sp.dma_start(d["states"], states[:]).then_inc(stored[0], 16)
                sp.wait_ge(stored[0], 16 * (CT // 2 + 1))
                sp.wait_ge(stored[1], 16 * (CT // 2))

            @block.tensor
            def _(pe):
                pe.wait_ge(w_loaded, 32)
                for ct in range(CT):
                    pe.wait_ge(x_loaded[ct % 2], ct // 2 * 16 + 16)
                    for dg in range(4):
                        for b, (s, w) in enumerate(TOKEN_BLOCKS):
                            n = (ct * 4 + dg) * NB + b
                            if n >= 8:
                                pe.wait_ge(gate_done, n - 7)
                            pe.matmul(banks[:, n % 8, :w], gate_w[:, dg * CT + ct, :], x[:, ct % 2, s:s + w],
                                      start=True, stop=True).then_inc(gate_mm, 1)

            @block.scalar
            def _(act):
                def gates(ct):
                    if ct >= 2:
                        act.wait_ge(input_ready, 2 * (ct - 1))
                    for dg in range(4):
                        direction, gate = dg // 2, dg % 2
                        for b, (s, w) in enumerate(TOKEN_BLOCKS):
                            n = (ct * 4 + dg) * NB + b
                            act.wait_ge(gate_mm, n + 1)
                            nc.scalar.activation((r, i)[gate][:, ct % 2, direction, s:s + w], banks[:, n % 8, :w],
                                                 ACT.Sigmoid,
                                                 bias=params[:, gb0 + dg * CT + ct:gb0 + dg * CT + ct + 1])\
                              .then_inc(gate_done, 1)

                def decays(ct):
                    if ct >= 2:
                        act.wait_ge(scanned, 4 * (ct - 1))
                    act.wait_ge(gate_done, (ct + 1) * 4 * NB)
                    for direction in range(2):
                        at = direction * CT + ct
                        n = 2 * ct + direction
                        gate = r[:, ct % 2, direction]
                        nc.scalar.activation(a[:, ct % 2, direction], gate, ACT.Exp,
                                             scale=keep["nsp8"][:, at:at + 1]).then_inc(decay_done, 1)
                        act.wait_ge(decay_done, 2 * n + 1)
                        nc.scalar.activation(gate, gate, ACT.Tanh, scale=keep["sp8"][:, at:at + 1]).then_inc(decay_done, 1)

                def roots(ct):
                    for direction in range(2):
                        act.wait_ge(one_minus, 2 * ct + direction + 1)
                        nc.scalar.activation(s2[:, ct % 2, direction], s2[:, ct % 2, direction],
                                             ACT.Sqrt).then_inc(root_done, 1)

                gates(0)
                for ct in range(CT):
                    decays(ct)
                    if ct + 1 < CT:
                        gates(ct + 1)
                    roots(ct)

            @block.gpsimd
            def _(pool):
                nc.gpsimd.memset(gate_w[:], 0.0).then_inc(zeroed, 1)
                for ct in range(CT):
                    for direction in range(2):
                        n = 2 * ct + direction
                        if ct >= 2:
                            pool.wait_ge(stored[ct % 2], 16 * (ct // 2))
                        pool.wait_ge(decay_done, 2 * n + 1)
                        nc.gpsimd.tensor_tensor(s2[:, ct % 2, direction], a[:, ct % 2, direction], a[:, ct % 2, direction],
                                                ALU.mult).then_inc(squared, 1)
                        nc.gpsimd.tensor_tensor(i[:, ct % 2, direction], i[:, ct % 2, direction], x[:, ct % 2],
                                                ALU.mult).then_inc(gated, 1)

            @block.vector
            def _(dve):
                def one_less_squares(ct):
                    for direction in range(2):
                        n = 2 * ct + direction
                        dve.wait_ge(decay_done, 2 * n + 2)
                        dve.wait_ge(squared, n + 1)
                        square = s2[:, ct % 2, direction]
                        nc.vector.scalar_tensor_tensor(out=square, in0=square, scalar=1.0, in1=r[:, ct % 2, direction],
                                                       op0=ALU.add, op1=ALU.mult).then_inc(one_minus, 1)

                def scans(ct):
                    for direction in range(2):
                        n = 2 * ct + direction
                        dve.wait_ge(gated, n + 1)
                        dve.wait_ge(root_done, n + 1)
                        nc.vector.tensor_tensor(s2[:, ct % 2, direction], s2[:, ct % 2, direction],
                                                i[:, ct % 2, direction], ALU.mult).then_inc(input_ready, 1)
                        dve.wait_ge(input_ready, n + 1)
                        h0 = params[:, h00 + direction * CT + ct:h00 + direction * CT + ct + 1]
                        for lo, hi, start in ((0, CTX_AT, h0), (CTX_AT, T, 0.0)):
                            views = [t[:, ct % 2, direction, lo:hi] for t in (s2, a, s2)]
                            if direction:
                                views = [v[:, ::-1] for v in views]
                            nc.vector.tensor_tensor_scan(*views, start, ALU.mult, ALU.add).then_inc(scanned, 1)
                        dve.wait_ge(scanned, 2 * n + 2)
                        end = T - 1 if direction == 0 else CTX_AT
                        nc.vector.tensor_copy(states[:, ct, direction:direction + 1],
                                              s2[:, ct % 2, direction, end:end + 1]).then_inc(state_done, 1)
                    dve.wait_ge(state_done, 2 * ct + 2)
                    dve.wait_ge(y_loaded[ct % 2], ct // 2 * 16 + 16)
                    result = s2[:, ct % 2, 0]
                    nc.vector.tensor_tensor(result, result, s2[:, ct % 2, 1], ALU.add).then_inc(summed, 1)
                    dve.wait_ge(summed, ct + 1)
                    nc.vector.tensor_tensor(result, result, gy[:, ct % 2], ALU.mult).then_inc(out_ready, 1)

                for ct in range(CT):
                    one_less_squares(ct)
                    scans(ct)

def interleave(*lists):
    keyed = [((i + 0.5) / len(x), n, i) for n, x in enumerate(lists) for i in range(len(x))]
    return [lists[n][i] for _, n, i in sorted(keyed)]


CONV_FORWARD = ([("turn_rows", j) for j in range(4)] + [("first", j) for j in range(8)]
                + [("turn_back", j) for j in range(8)] + [("second", j) for j in range(8)])
CONV_BACK = ([("back1", j) for j in range(8)] + [("turn_pairs", j) for j in range(8)]
             + [("back2", j) for j in range(4)])
FILTER_FIRST = [x for j in range(8) for x in (("taps", j), ("f_first", j))]
FILTER_SECOND = [x for j in range(8) for x in (("f_turn_back", j), ("f_second", j))]
CTX_FORWARD = [("ctx_turn", 0), ("ctx_forward", 0)]
CTX_BACK = [("ctx_back", 0)]
CTX_TAPS, CTX_FILTER = [("ctx_taps", 0)], [("ctx_filter", 0)]
BATCHES = {"turn_rows": 4, "first": 8, "turn_back": 8, "second": 8, "back1": 8, "turn_pairs": 8, "back2": 4,
           "taps": 8, "f_first": 8, "f_turn_back": 8, "f_second": 8,
           "ctx_turn": 1, "ctx_forward": 1, "ctx_back": 1, "ctx_taps": 1, "ctx_filter": 1}
ONLY_FILTER = FILTER_FIRST[:8] + CTX_TAPS + FILTER_FIRST[8:] + FILTER_SECOND + CTX_FILTER
ONLY_CONV = interleave(CONV_FORWARD, CTX_FORWARD) + interleave(CONV_BACK, CTX_BACK)
BOTH = (interleave(CONV_FORWARD, FILTER_FIRST, [CTX_FORWARD[0], CTX_TAPS[0], CTX_FORWARD[1]])
        + interleave(CONV_BACK, FILTER_SECOND, [CTX_BACK[0], CTX_FILTER[0]]))
CONV_CHAIN = CONV_FORWARD + CONV_BACK


def hyena(nc, sem, d, keep):
    with ExitStack() as ctx:
        def sb(name, shape, dt=F32):
            return ctx.enter_context(nc.sbuf_tensor(name, shape, dt))

        hidden = sb("hy_hidden", [P, POS])
        first_t, second_t = sb("first_table", [P, 2, 256]), sb("second_table", [P, 32, P])
        back1_t, back2_t = sb("back1_table", [P, 32, P]), sb("back2_table", [P, 64])
        ctx_fwd, ctx_inv = sb("ctx_forward_table", [P, 2, 2, P]), sb("ctx_back_table", [P, 2, P])
        decay = sb("decay", [P, ROW_TILES, P])
        w3 = sb("mlp_w3", [P, 2, 2, P])
        z = sb("hy_z", [P, T])
        gates = sb("hy_gates", [P, 2, T])
        rows = sb("hy_rows", [P, 16, P])
        spectrum_c = sb("hy_by_channel", [P, 64, 64])
        spectrum_p = sb("hy_by_slot", [P, 32, P])
        swapped = sb("hy_swapped", [P, 2, 4, P])
        gated = rows[:, 0:8].rearrange("p (j q) c -> p j (q c)", j=2)
        taps = sb("taps", [P, 2, 4, P])
        f_by_channel = sb("f_by_channel", [P, 64, 64])
        f_by_slot = sb("f_by_slot", [P, 2, 4, P])
        f_re, f_im = sb("filter_re", [P, 32, P]), sb("filter_im", [P, 32, P])
        ctx_rows, ctx_y, ctx_tmp = sb("ctx_rows", [P, P]), sb("ctx_y", [P, 2, P]), sb("ctx_tmp", [P, 2, P])
        ctx_taps, ctx_f = sb("ctx_taps", [P, 2, P]), sb("ctx_f", [P, 3, P])
        conv_bank = ctx.enter_context(nc.psum_tensor("conv_bank", [P, 4, 512], F32))
        filter_bank = ctx.enter_context(nc.psum_tensor("filter_bank", [P, 2, 512], F32))
        ctx_bank = ctx.enter_context(nc.psum_tensor("ctx_bank", [P, 2, 512], F32))

        mm = {q: sem(f"{q}_mm") for q in BATCHES}
        out = {q: sem(f"{q}_out") for q in BATCHES}
        tables_loaded, w3_zeroed = sem("hy_tables_loaded"), sem("w3_zeroed")
        z_loaded, gates_loaded, z_stored = sem("hy_z_loaded"), sem("hy_gates_loaded"), sem("hy_z_stored")
        decay_loaded, w3_loaded = sem("decay_loaded"), sem("w3_loaded")
        swap_ready, cross_ready, slots_ready = sem("swap_ready"), sem("cross_ready"), sem("slots_ready")
        re_ready, im_step = sem("filter_re_ready"), sem("filter_im_step")
        biased, ctx_step, ctx_biased, ctx_copied = (sem(q) for q in ("hy_biased", "ctx_step", "ctx_biased", "ctx_copied"))
        params, ident = keep["params"], keep["ident"]
        hb0 = PARAMS["hy_b"][0]

        def each_turn(engine, batch, both=True):
            for stage, j in ONLY_FILTER:
                batch(stage, j, 0, 0, None, 0)
            with engine.Fori(0, CT - 1) as ct:
                for order in range(2):
                    for stage, j in BOTH:
                        batch(stage, j, ct, order, ct * 2 + order, ct * 2 + (order + 1))
            for order in range(2):
                for stage, j in (BOTH, ONLY_CONV)[order]:
                    batch(stage, j, CT - 1, order, 2 * (CT - 1) + order, 2 * (CT - 1) + order + 1)

        with nc.Block() as block:
            @block.sync
            def _(sp):
                def load_filter_inputs(ct):
                    sp.dma_start(decay[:], d["decay"][ct]).then_inc(decay_loaded, 16)
                    for order in range(2):
                        sp.dma_start(w3[0:64, order], d["mlp_w3"][order][ct]).then_inc(w3_loaded, 16)

                def load_conv_inputs(ct):
                    sp.dma_start(z[:], d["pre"][ct + CT]).then_inc(z_loaded, 16)
                    for order in range(2):
                        sp.dma_start(gates[:, order], d["pre"][ct + (2 + order) * CT]).then_inc(gates_loaded, 16)

                sp.wait_ge(w3_zeroed, 1)
                sp.dma_start(hidden[:], d["hidden"]).then_inc(tables_loaded, 16)
                load_filter_inputs(0)
                for dst, src in ((first_t, "first_table"), (second_t, "second_table"), (ctx_fwd, "ctx_forward_table"),
                                 (back1_t, "back1_table"), (back2_t, "back2_table"), (ctx_inv, "ctx_back_table")):
                    sp.dma_start(dst[:], d[src]).then_inc(tables_loaded, 16)
                load_conv_inputs(0)

                def finish(ct):
                    sp.wait_ge(out["back2"], ct * 8 + 8)
                    sp.wait_ge(out["ctx_back"], ct * 2 + 2)
                    sp.dma_start(d["mixed"][ct + CT], z[:]).then_inc(z_stored, 16)

                with sp.Fori(0, CT - 1) as ct:
                    sp.wait_ge(out["taps"], ct * 16 + 16)
                    sp.wait_ge(out["ctx_taps"], ct * 2 + 2)
                    load_filter_inputs(ct + 1)
                    finish(ct)
                    sp.wait_ge(z_stored, ct * 16 + 16)
                    load_conv_inputs(ct + 1)
                finish(CT - 1)
                sp.wait_ge(z_stored, 16 * CT)

            @block.tensor
            def _(pe):
                def batch(stage, j, ct, order, turn, f_turn):
                    if (stage, j) in CONV_CHAIN:
                        at = CONV_CHAIN.index((stage, j))
                        bank = conv_bank[:, at % 4, :]
                        if at >= 4:
                            before, jb = CONV_CHAIN[at - 4]
                            pe.wait_ge(out[before], turn * BATCHES[before] + jb + 1)
                    four = lambda t: t.rearrange("p (q c) -> p q c", q=4)
                    if stage == "turn_rows":
                        if j == 0:
                            if order == 0:
                                pe.wait_ge(z_loaded, ct * 16 + 16)
                            else:
                                pe.wait_ge(out["back2"], turn * 4)
                        for q in range(4):
                            last = pe.transpose(four(bank)[:, q], z[:, 4 * j + q:SEQ_LAT:16], ident[:])
                    elif stage == "first":
                        pe.wait_ge(out["turn_rows"], turn * 4 + j // 2 + 1)
                        for q in range(2):
                            last = pe.matmul(bank[:, 256 * q:256 * q + 256], rows[:, 2 * j + q], first_t[:, 0],
                                             start=True, stop=True)
                    elif stage == "turn_back":
                        if j == 0:
                            pe.wait_ge(out["first"], turn * 8 + 8)
                        for q in range(4):
                            g = 4 * j + q
                            last = pe.transpose(four(bank)[:, q], spectrum_c[:, 2 * g:2 * g + 2, :]
                                                .rearrange("p r b -> p (r b)"), ident[:])
                    elif stage == "second":
                        pe.wait_ge(out["turn_back"], turn * 8 + j + 1)
                        for q in range(4):
                            g = 4 * j + q
                            last = pe.matmul(four(bank)[:, q], second_t[:, g], spectrum_p[:, g], start=True, stop=True)
                    elif stage == "back1":
                        pe.wait_ge(slots_ready, turn * 8 + j + 1)
                        for q in range(4):
                            g = 4 * j + q
                            last = pe.matmul(four(bank)[:, q], spectrum_p[:, g], back1_t[:, g], start=True, stop=True)
                    elif stage == "turn_pairs":
                        if j == 0:
                            pe.wait_ge(out["back1"], turn * 8 + 8)
                        flat = spectrum_c[:].rearrange("p r b -> p (r b)")
                        for q in range(4):
                            g = 4 * j + q
                            last = pe.transpose(four(bank)[:, q], flat[:, g:4096:32], ident[:])
                    elif stage == "back2":
                        pe.wait_ge(out["turn_pairs"], turn * 8 + 2 * j + 2)
                        for q in range(8):
                            last = pe.matmul(bank[:, 64 * q:64 * q + 64], spectrum_p[:, 8 * j + q], back2_t[:],
                                             start=True, stop=True)
                    elif stage == "taps":
                        if j == 0:
                            pe.wait_ge(w3_loaded, f_ct(order, turn, ct) * 32 + 32)
                            if turn is None:
                                pe.wait_ge(tables_loaded, 16 * 7)
                            else:
                                pe.wait_ge(out["f_turn_back"], f_turn * 8)
                        else:
                            pe.wait_ge(out["taps"], f_turn * 8 + j)
                        for q in range(4):
                            rt = 4 * j + q
                            last = pe.matmul(four(filter_bank[:, 0])[:, q], hidden[:, rt * P:rt * P + P],
                                             w3[:, f_order(order, turn), q % 2], start=True, stop=True)
                    elif stage == "f_first":
                        pe.wait_ge(out["taps"], f_turn * 8 + j + 1)
                        if j == 0 and turn is not None:
                            pe.wait_ge(out["f_second"], f_turn * 8)
                        elif j:
                            pe.wait_ge(out["f_first"], f_turn * 8 + j)
                        for q in range(2):
                            for half in range(2):
                                last = pe.matmul(filter_bank[:, 1, 256 * q:256 * q + 256], taps[:, j % 2, 2 * q + half],
                                                 first_t[:, half], start=(half == 0), stop=(half == 1))
                    elif stage == "f_turn_back":
                        if j == 0:
                            pe.wait_ge(out["f_first"], f_turn * 8 + 8)
                            pe.wait_ge(out["taps"], f_turn * 8 + 8)
                        else:
                            pe.wait_ge(out["f_turn_back"], f_turn * 8 + j)
                        for q in range(4):
                            g = 4 * j + q
                            last = pe.transpose(four(filter_bank[:, 0])[:, q], f_by_channel[:, 2 * g:2 * g + 2, :]
                                                .rearrange("p r b -> p (r b)"), ident[:])
                    elif stage == "f_second":
                        pe.wait_ge(out["f_turn_back"], f_turn * 8 + j + 1)
                        if j:
                            pe.wait_ge(out["f_second"], f_turn * 8 + j)
                        for q in range(4):
                            last = pe.matmul(four(filter_bank[:, 1])[:, q], second_t[:, 4 * j + q], f_by_slot[:, j % 2, q],
                                             start=True, stop=True)
                    elif stage == "ctx_turn":
                        if order == 0:
                            pe.wait_ge(z_loaded, ct * 16 + 16)
                        else:
                            pe.wait_ge(out["ctx_back"], turn)
                        pe.wait_ge(out["ctx_filter"], turn + 1)
                        last = pe.transpose(ctx_bank[:, 0, :P], z[:, CTX_AT:T], ident[:])
                    elif stage == "ctx_forward":
                        pe.wait_ge(out["ctx_turn"], turn + 1)
                        for part in range(2):
                            last = pe.matmul(ctx_bank[:, 0, P * part:P * part + P], ctx_fwd[:, 0, part], ctx_rows[:],
                                             start=True, stop=True)
                    elif stage == "ctx_back":
                        pe.wait_ge(out["ctx_forward"], turn + 1)
                        pe.wait_ge(out["ctx_taps"], turn + 1)
                        for part in range(2):
                            last = pe.matmul(ctx_bank[:, 1, :P], ctx_y[:, part], ctx_inv[:, part],
                                             start=(part == 0), stop=(part == 1))
                    elif stage == "ctx_taps":
                        if order == 1:
                            pe.wait_ge(out["ctx_back"], turn)
                        for half in range(2):
                            last = pe.matmul(ctx_bank[:, 1, P * half:P * half + P],
                                             hidden[:, POS_LAT + half * P:POS_LAT + half * P + P],
                                             w3[:, f_order(order, turn), half], start=True, stop=True)
                    elif stage == "ctx_filter":
                        pe.wait_ge(out["ctx_taps"], f_turn + 1)
                        if turn is not None:
                            pe.wait_ge(out["ctx_forward"], turn + 1)
                        for part in range(2):
                            for half in range(2):
                                last = pe.matmul(ctx_bank[:, 0, P * part:P * part + P], ctx_fwd[:, half, part],
                                                 ctx_taps[:, half], start=(half == 0), stop=(half == 1))
                    last.then_inc(mm[stage], 1)

                each_turn(pe, batch)

            @block.scalar
            def _(act):
                def batch(stage, j, ct, order, turn, f_turn):
                    at = CONV_CHAIN.index((stage, j)) if (stage, j) in CONV_CHAIN else 0
                    bank = conv_bank[:, at % 4, :]
                    if stage == "turn_rows":
                        act.wait_ge(mm[stage], turn * 4 + j + 1)
                        nc.scalar.activation(rows[:, 4 * j:4 * j + 4].rearrange("p q c -> p (q c)"), bank,
                                             ACT.Copy).then_inc(out[stage], 1)
                    elif stage in ("first", "f_first"):
                        t, source, by_channel = ((turn, bank, spectrum_c) if stage == "first"
                                                 else (f_turn, filter_bank[:, 1], f_by_channel))
                        act.wait_ge(mm[stage], t * 8 + j + 1)
                        for q in range(2):
                            last = nc.scalar.activation(by_channel[:, :, 8 * j + 4 * q:8 * j + 4 * q + 4],
                                                        source[:, 256 * q:256 * q + 256].rearrange("p (r b) -> p r b", b=4),
                                                        ACT.Copy)
                        last.then_inc(out[stage], 1)
                    elif stage == "second":
                        act.wait_ge(mm[stage], turn * 8 + j + 1)
                        if j >= 2:
                            act.wait_ge(slots_ready, turn * 8 + j - 1)
                        to = swapped[:, j % 2].rearrange("p q c -> p (q c)")
                        nc.scalar.activation(to[0:64], bank[64:128], ACT.Copy)
                        nc.scalar.activation(to[64:128], bank[0:64], ACT.Copy).then_inc(swap_ready, 1)
                    elif stage == "back1":
                        act.wait_ge(mm[stage], turn * 8 + j + 1)
                        nc.scalar.activation(spectrum_c[:, 8 * j:8 * j + 8, :].rearrange("p r b -> p (r b)"), bank,
                                             ACT.Copy).then_inc(out[stage], 1)
                    elif stage == "f_second":
                        act.wait_ge(mm[stage], f_turn * 8 + j + 1)
                        to = f_re[:, 4 * j:4 * j + 4].rearrange("p q c -> p (q c)")
                        nc.scalar.activation(to[0:64], filter_bank[0:64, 1], ACT.Copy)
                        last = nc.scalar.activation(to[64:128], filter_bank[0:64, 1], ACT.Copy).then_inc(re_ready, 1)
                        if j == 0:
                            act.wait_ge(re_ready, f_turn * 9 + 1)
                            nc.scalar.activation(f_re[96:97, 0], filter_bank[96:97, 1, 0:P], ACT.Copy).then_inc(re_ready, 1)
                    elif stage == "ctx_turn":
                        act.wait_ge(mm[stage], turn + 1)
                        nc.scalar.activation(ctx_rows[:], ctx_bank[:, 0, :P], ACT.Copy).then_inc(out[stage], 1)
                    elif stage == "ctx_filter":
                        act.wait_ge(mm[stage], f_turn + 1)
                        nc.scalar.activation(ctx_f[:, 0], ctx_bank[:, 0, 0:P], ACT.Copy)
                        nc.scalar.activation(ctx_f[:, 1], ctx_bank[:, 0, P:2 * P], ACT.Copy)
                        nc.scalar.activation(ctx_f[:, 2], ctx_bank[:, 0, 0:P], ACT.Copy).then_inc(ctx_copied, 1)
                        act.wait_ge(ctx_copied, f_turn * 2 + 1)
                        nc.scalar.activation(ctx_f[0:1, 2], ctx_f[0:1, 1], ACT.Copy).then_inc(ctx_copied, 1)
                        act.wait_ge(ctx_copied, f_turn * 2 + 2)
                        nc.scalar.activation(ctx_f[0:1, 1], ctx_f[0:1, 1], ACT.Copy, scale=0.0).then_inc(out[stage], 1)

                each_turn(act, batch)

            @block.gpsimd
            def _(pool):
                nc.gpsimd.memset(w3[:], 0.0).then_inc(w3_zeroed, 1)

                def batch(stage, j, ct, order, turn, f_turn):
                    if stage == "second":
                        pool.wait_ge(swap_ready, turn * 8 + j + 1)
                        nc.gpsimd.tensor_tensor(swapped[:, j % 2], swapped[:, j % 2], f_im[:, 4 * j:4 * j + 4],
                                                ALU.mult).then_inc(cross_ready, 1)
                    elif stage == "back2":
                        if j == 0:
                            pool.wait_ge(gates_loaded, ct * 32 + 32)
                        pool.wait_ge(biased, turn * 4 + j + 1)
                        at = slice(8 * j, 8 * j + 8)
                        view = lambda t: t.rearrange("p (m b) -> p m b", b=32)[:, :, at]
                        nc.gpsimd.tensor_tensor(view(z[:, :SEQ_LAT]), gated[:, j % 2].rearrange("p (m b) -> p m b", b=8),
                                                view(gates[:, order, :SEQ_LAT]), ALU.mult).then_inc(out[stage], 1)

                each_turn(pool, batch)

            @block.vector
            def _(dve):
                def batch(stage, j, ct, order, turn, f_turn):
                    at = CONV_CHAIN.index((stage, j)) if (stage, j) in CONV_CHAIN else 0
                    bank = conv_bank[:, at % 4, :]
                    bias = params[:, bass.ds(ct + (hb0 + order * CT), 1)]
                    flat4 = lambda t: t.rearrange("p q c -> p (q c)")
                    if stage in ("turn_back", "turn_pairs"):
                        dve.wait_ge(mm[stage], turn * 8 + j + 1)
                        nc.vector.tensor_copy(flat4(spectrum_p[:, 4 * j:4 * j + 4]), bank).then_inc(out[stage], 1)
                    elif stage == "second":
                        dve.wait_ge(swap_ready, turn * 8 + j + 1)
                        nc.vector.tensor_tensor(flat4(spectrum_p[:, 4 * j:4 * j + 4]), bank, flat4(f_re[:, 4 * j:4 * j + 4]),
                                                ALU.mult).then_inc(out[stage], 1)
                        dve.wait_ge(out[stage], turn * 8 + j + 1)
                        dve.wait_ge(cross_ready, turn * 8 + j + 1)
                        nc.vector.tensor_tensor(spectrum_p[:, 4 * j:4 * j + 4], spectrum_p[:, 4 * j:4 * j + 4],
                                                swapped[:, j % 2], ALU.add).then_inc(slots_ready, 1)
                    elif stage == "back2":
                        dve.wait_ge(mm[stage], turn * 4 + j + 1)
                        if j >= 2:
                            dve.wait_ge(out[stage], turn * 4 + j - 1)
                        nc.vector.scalar_tensor_tensor(
                            out=gated[:, j % 2].rearrange("p (m b) -> p m b", b=8),
                            in0=z[:, :SEQ_LAT].rearrange("p (m b) -> p m b", b=32)[:, :, 8 * j:8 * j + 8], scalar=bias,
                            in1=bank.rearrange("p (b m) -> p m b", b=8), op0=ALU.mult, op1=ALU.add).then_inc(biased, 1)
                    elif stage == "taps":
                        if j == 0:
                            dve.wait_ge(decay_loaded, f_ct(order, turn, ct) * 16 + 16)
                        dve.wait_ge(mm[stage], f_turn * 8 + j + 1)
                        if j >= 2:
                            dve.wait_ge(mm["f_first"], f_turn * 8 + j - 1)
                        nc.vector.tensor_tensor(flat4(taps[:, j % 2]), filter_bank[:, 0], flat4(decay[:, 4 * j:4 * j + 4]),
                                                ALU.mult).then_inc(out[stage], 1)
                    elif stage == "f_turn_back":
                        dve.wait_ge(mm[stage], f_turn * 8 + j + 1)
                        if j >= 2:
                            dve.wait_ge(mm["f_second"], f_turn * 8 + j - 1)
                        nc.vector.tensor_copy(flat4(f_by_slot[:, j % 2]), filter_bank[:, 0]).then_inc(out[stage], 1)
                    elif stage == "f_second":
                        dve.wait_ge(re_ready, f_turn * 9 + j + 2)
                        to = flat4(f_im[:, 4 * j:4 * j + 4])
                        nc.vector.tensor_copy(to[64:128], filter_bank[64:128, 1])
                        last = nc.vector.tensor_scalar(to[0:64], filter_bank[64:128, 1], -1.0, None, ALU.mult)
                        if j == 0:
                            last.then_inc(im_step, 1)
                            dve.wait_ge(im_step, f_turn * 2 + 1)
                            nc.vector.memset(f_im[32:33, 0], 0.0)
                            nc.vector.memset(f_im[96:97, 0], 0.0).then_inc(im_step, 1)
                            dve.wait_ge(im_step, f_turn * 2 + 2)
                            dve.sem_inc(out[stage], 1)
                        else:
                            last.then_inc(out[stage], 1)
                    elif stage == "ctx_taps":
                        dve.wait_ge(mm[stage], f_turn + 1)
                        nc.vector.tensor_tensor(flat4(ctx_taps[:]), ctx_bank[:, 1, 0:2 * P], flat4(decay[:, 32:34]),
                                                ALU.mult).then_inc(out[stage], 1)
                    elif stage == "ctx_forward":
                        dve.wait_ge(mm[stage], turn + 1)
                        u_re, u_im = ctx_bank[:, 0, 0:P], ctx_bank[:, 0, P:2 * P]
                        for part, (p, q, op) in enumerate(((0, 1, ALU.subtract), (1, 2, ALU.add))):
                            done = turn * 4 + 2 * part
                            nc.vector.tensor_tensor(ctx_y[:, part], u_re, ctx_f[:, p], ALU.mult)
                            nc.vector.tensor_tensor(ctx_tmp[:, part], u_im, ctx_f[:, q], ALU.mult).then_inc(ctx_step, 1)
                            dve.wait_ge(ctx_step, done + 1)
                            last = nc.vector.tensor_tensor(ctx_y[:, part], ctx_y[:, part], ctx_tmp[:, part], op)
                            last.then_inc(ctx_step, 1)
                        dve.wait_ge(ctx_step, turn * 4 + 4)
                        dve.sem_inc(out[stage], 1)
                    elif stage == "ctx_back":
                        dve.wait_ge(mm[stage], turn + 1)
                        dve.wait_ge(gates_loaded, ct * 32 + 32)
                        nc.vector.scalar_tensor_tensor(out=ctx_tmp[:, 0], in0=z[:, CTX_AT:], scalar=bias,
                                                       in1=ctx_bank[:, 1, :P], op0=ALU.mult, op1=ALU.add).then_inc(ctx_biased, 1)
                        dve.wait_ge(ctx_biased, turn + 1)
                        nc.vector.tensor_tensor(z[:, CTX_AT:], ctx_tmp[:, 0], gates[:, order, CTX_AT:],
                                                ALU.mult).then_inc(out[stage], 1)

                each_turn(dve, batch)


def f_order(order, turn):
    return 0 if turn is None else 1 - order


def f_ct(order, turn, ct):
    return 0 if turn is None else ct + order


def out_proj(nc, sem, d, keep):
    with ExitStack() as ctx:
        def sb(name, shape, dt=F32):
            return ctx.enter_context(nc.sbuf_tensor(name, shape, dt))

        def psum(name, shape, dt=F32):
            return ctx.enter_context(nc.psum_tensor(name, shape, dt))

        xh, xl = sb("oh", [P, KM, T], F32R), sb("ol", [P, KM, T], F32R)
        x = sb("residual", [P, 2, T])
        norm_banks, banks = psum("out_norm_banks", [P, 3, 512]), psum("out_banks", [P, NB, 512])
        nb = norm_buffers(sb, keep["norm_sems"], "out", 2, norm_banks[:, 0], [norm_banks[:, 1], norm_banks[:, 2]],
                          x[:, 1])
        wb = weight_buffers(sb, sem, keep["zero"], "out")
        bank_free, added, stored = sem("out_bank_free"), sem("out_added"), sem("out_stored")
        x_loaded = [sem("residual_loaded0"), sem("residual_loaded1")]
        params, mod = keep["params"], keep["mod"]
        go0 = PARAMS["go"][0]
        gain = params[:, go0:go0 + KM].unsqueeze(2).broadcast_to([P, KM, 2])

        with nc.Block() as block:
            @block.sync
            def _(sp):
                norm_load(sp, nb, d["mixed"], 0)
                sp.dma_start(wb["whole"][:], d["w_out"][0]).then_inc(wb["loaded"], 16)
                norm_load(sp, nb, d["mixed"], 1)
                sp.wait_ge(wb["ready"], 1)
                sp.dma_start(wb["whole"][:], d["w_out"][1]).then_inc(wb["loaded"], 16)
                for b in range(2, NNB):
                    norm_load(sp, nb, d["mixed"], b)
                for n in range(KM):
                    if n == 1:
                        norm_wait(sp, nb, "scaled_ready", KM * NNB)
                    if n >= 2:
                        sp.wait_ge(wb["ready"], n)
                        sp.dma_start(wb["whole"][:], d["w_out"][n]).then_inc(wb["loaded"], 16)
                    if n >= 2:
                        sp.wait_ge(added, (n - 1) * NB)
                        sp.dma_start(d["x1"][n - 2], x[:, n % 2]).then_inc(stored, 16)
                        sp.wait_ge(stored, 16 * (n - 1))
                    sp.dma_start(x[:, n % 2], d["xT"][n]).then_inc(x_loaded[n % 2], 16)
                for n in (KM - 2, KM - 1):
                    sp.wait_ge(added, (n + 1) * NB)
                    sp.dma_start(d["x1"][n], x[:, n % 2]).then_inc(stored, 16)
                sp.wait_ge(stored, 16 * KM)

            @block.scalar
            def _(act):
                norm_scalar(nc, act, nb, None, xh)

            @block.gpsimd
            def _(pool):
                norm_and_weight_splits(nc, pool, nb, wb, KM)

            @block.tensor
            def _(pe):
                def first_product(b):
                    s, w = TOKEN_BLOCKS[b]
                    if b == 0:
                        pe.wait_ge(wb["ready"], 1)
                    wait_for_block(pe, nb, b)
                    product_block(pe, banks[:, b, :w], wb, 0, xh, xl, s, w)

                norm_tensor(pe, nb, keep["ones"], keep["ident"], first_product)
                for n in range(1, KM):
                    pe.wait_ge(wb["ready"], n + 1)
                    for b, (s, w) in enumerate(TOKEN_BLOCKS):
                        pe.wait_ge(added, (n - 1) * NB + b + 1)
                        product_block(pe, banks[:, b, :w], wb, n % 2, xh, xl, s, w)

            @block.vector
            def _(dve):
                norm_vector(nc, dve, nb, gain, None, xh, xl)
                for n in range(KM):
                    dve.wait_ge(x_loaded[n % 2], n // 2 * 16 + 16)
                    for b, (s, w) in enumerate(TOKEN_BLOCKS):
                        dve.wait_ge(wb["block_done"], n * NB + b + 1)
                        for at, width, m in segments(s, w):
                            last = nc.vector.scalar_tensor_tensor(
                                out=x[:, n % 2, at:at + width], in0=banks[:, b, at - s:at - s + width],
                                scalar=mod[:, GATE1 + n, m:m + 1], in1=x[:, n % 2, at:at + width],
                                op0=ALU.mult, op1=ALU.add)
                        last.then_inc(added, 1)


def ffn_up(nc, sem, d, keep):
    pitch = GRID_W + 2
    with ExitStack() as ctx:
        def sb(name, shape, dt=F32):
            return ctx.enter_context(nc.sbuf_tensor(name, shape, dt))

        def psum(name, shape, dt=F32):
            return ctx.enter_context(nc.psum_tensor(name, shape, dt))

        xh, xl = sb("xh2", [P, KM, T], F32R), sb("xl2", [P, KM, T], F32R)
        h = sb("ffn_hidden", [P, T])
        sum_bank, gate_bank = psum("up_sum_bank", [P, 512]), psum("gate_bank", [P, 2, 512])
        nb = norm_buffers(sb, keep["norm_sems"], "up", 1, sum_bank[:], [gate_bank[:, 0], gate_bank[:, 1]], h)
        wb = weight_buffers(sb, sem, keep["zero"], "up")
        grid = sb("grid", [P, GRID_H + 2, pitch])
        line = sb("line", [P, SEQ_CTX + 2])
        factor_bank = psum("factor_bank", [P, NB, 512])
        borders_zero, gate_out, factor_free, tap_done, conv_ready, gelu_ready, h_ready, h_stored = (
            sem("up_" + q) for q in ("borders_zero", "gate_out", "factor_free", "tap_done", "conv_ready",
                                     "gelu_ready", "h_ready", "h_stored"))
        params = keep["params"]
        shift = keep["mod"][:, SHIFT2:SHIFT2 + KM, :]
        fw0, fb0 = PARAMS["ffn_w"][0], PARAMS["ffn_b"][0]
        taps = [(dy, dx) for dy in range(3) for dx in range(3)]

        with nc.Block() as block:
            @block.sync
            def _(sp):
                norm_load(sp, nb, d["x1"], 0)
                sp.dma_start(wb["whole"][:], d["w_up"][0]).then_inc(wb["loaded"], 16)
                norm_load(sp, nb, d["x1"], 1)
                sp.wait_ge(wb["ready"], 1)
                sp.dma_start(wb["whole"][:], d["w_up"][1]).then_inc(wb["loaded"], 16)
                for b in range(2, NNB):
                    norm_load(sp, nb, d["x1"], b)
                with sp.Fori(1, KF) as f:
                    for u in range(2):
                        sp.wait_ge(wb["ready"], f * 2 + u)
                        sp.dma_start(wb["whole"][:], d["w_up"][f * 2 + u]).then_inc(wb["loaded"], 16)
                    sp.wait_ge(h_ready, f)
                    sp.dma_start(d["hidden_ff"][f - 1], h[:]).then_inc(h_stored, 16)
                sp.wait_ge(h_ready, KF)
                sp.dma_start(d["hidden_ff"][KF - 1], h[:]).then_inc(h_stored, 16)
                sp.wait_ge(h_stored, 16 * (KF + 1))

            @block.scalar
            def _(act):
                norm_scalar(nc, act, nb, shift, xh)
                act.sem_inc(gate_out, 2)
                act.wait_ge(borders_zero, 2)

                def tile(f, gate_unit):
                    for b, (s, w) in enumerate(TOKEN_BLOCKS):
                        act.wait_ge(wb["block_done"], f * 2 * NB + (gate_unit * NB + b + 1))
                        for at, width, m in segments(s, w):
                            source = gate_bank[:, b % 2, at - s:at - s + width]
                            if m == LAT:
                                y = at // GRID_W + 1
                                last = nc.scalar.activation(grid[:, y:y + width // GRID_W, 1:1 + GRID_W],
                                                            source.rearrange("p (y x) -> p y x", x=GRID_W), ACT.Copy)
                            else:
                                last = nc.scalar.activation(line[:, 1:1 + SEQ_CTX], source, ACT.Copy)
                        last.then_inc(gate_out, 1)
                    act.wait_ge(conv_ready, f + 1)
                    nc.scalar.activation(h[:], h[:], ACT.Gelu_apprx_tanh).then_inc(gelu_ready, 1)

                tile(0, 1)
                with act.Fori(1, KF) as f:
                    tile(f, 0)

            @block.gpsimd
            def _(pool):
                nc.gpsimd.memset(grid[:], 0.0).then_inc(borders_zero, 1)
                nc.gpsimd.memset(line[:], 0.0).then_inc(borders_zero, 1)
                norm_and_weight_splits(nc, pool, nb, wb, 2 * KF)

            @block.vector
            def _(dve):
                norm_vector(nc, dve, nb, keep["scale2"], shift, xh, xl)
                dve.sem_inc(h_stored, 16)

                def tile(f, factor_unit):
                    own = Steps(dve, tap_done, f * (len(taps) - 1))
                    dve.wait_ge(gate_out, f * NB + (2 + NB))
                    dve.wait_ge(h_stored, f * 16 + 16)
                    for n, (dy, dx) in enumerate(taps):
                        weight = params[:, bass.ds(f + (fw0 + n * KF), 1)]
                        y = h[:, :SEQ_LAT].rearrange("p (y x) -> p y x", x=GRID_W)
                        window = grid[:, dy:dy + GRID_H, dx:dx + GRID_W]
                        if n == 0:
                            last = nc.vector.tensor_scalar(y, window, weight, params[:, bass.ds(f + fb0, 1)],
                                                           ALU.mult, ALU.add)
                        else:
                            last = nc.vector.scalar_tensor_tensor(out=y, in0=window, scalar=weight, in1=y,
                                                                  op0=ALU.mult, op1=ALU.add)
                        if dy == 1:
                            y, window = h[:, CTX_AT:], line[:, dx:dx + SEQ_CTX]
                            if dx == 0:
                                last = nc.vector.tensor_scalar(y, window, weight, params[:, bass.ds(f + fb0, 1)],
                                                               ALU.mult, ALU.add)
                            else:
                                last = nc.vector.scalar_tensor_tensor(out=y, in0=window, scalar=weight, in1=y,
                                                                      op0=ALU.mult, op1=ALU.add)
                        if n < len(taps) - 1:
                            own.done(last)
                            own.wait()
                        else:
                            last.then_inc(conv_ready, 1)
                    dve.wait_ge(gelu_ready, f + 1)
                    for b, (s, w) in enumerate(TOKEN_BLOCKS):
                        dve.wait_ge(wb["block_done"], f * 2 * NB + (factor_unit * NB + b + 1))
                        nc.vector.tensor_tensor(h[:, s:s + w], h[:, s:s + w], factor_bank[:, b, :w],
                                                ALU.mult).then_inc(factor_free, 1)
                    dve.wait_ge(factor_free, f * NB + NB)
                    dve.sem_inc(h_ready, 1)

                tile(0, 0)
                with dve.Fori(1, KF) as f:
                    tile(f, 1)

            @block.tensor
            def _(pe):
                def gate(f, u):
                    for b, (s, w) in enumerate(TOKEN_BLOCKS):
                        pe.wait_ge(gate_out, f * NB + max(2, b + 1))
                        product_block(pe, gate_bank[:, b % 2, :w], wb, u, xh, xl, s, w)

                def first_product(b):
                    s, w = TOKEN_BLOCKS[b]
                    if b == 0:
                        pe.wait_ge(wb["ready"], 1)
                    wait_for_block(pe, nb, b)
                    product_block(pe, factor_bank[:, b, :w], wb, 0, xh, xl, s, w)

                norm_tensor(pe, nb, keep["ones"], keep["ident"], first_product)
                pe.wait_ge(wb["ready"], 2)
                gate(0, 1)
                with pe.Fori(1, KF) as f:
                    pe.wait_ge(wb["ready"], f * 2 + 1)
                    gate(f, 0)
                    pe.wait_ge(wb["ready"], f * 2 + 2)
                    for b, (s, w) in enumerate(TOKEN_BLOCKS):
                        pe.wait_ge(factor_free, (f - 1) * NB + (b + 1))
                        product_block(pe, factor_bank[:, b, :w], wb, 1, xh, xl, s, w)


DOWN_W = 272
DOWN_BLOCKS = T // DOWN_W


def ffn_down(nc, sem, d, keep):
    with ExitStack() as ctx:
        def sb(name, shape, dt=F32):
            return ctx.enter_context(nc.sbuf_tensor(name, shape, dt))

        whole = sb("down_whole", [P, D_MODEL])
        wh, wl = sb("down_hi", [P, KF, D_MODEL], F32R), sb("down_lo", [P, KF, D_MODEL], F32R)
        h = sb("down_h", [P, 4, DOWN_W])
        hh, hl = sb("down_h_hi", [P, 2, DOWN_W], F32R), sb("down_h_lo", [P, 2, DOWN_W], F32R)
        x = sb("down_x", [P, KM, DOWN_W])
        square = sb("down_square", [P, DOWN_W])
        total, rstd = sb("down_total", [P, DOWN_W]), sb("down_rstd", [P, DOWN_W])
        banks = ctx.enter_context(nc.psum_tensor("down_banks", [P, KM, 512], F32))
        w_loaded = [sem(f"down_w_loaded{slot}") for slot in range(3)]
        w_hi, w_ready = sem("down_w_hi"), sem("down_w_ready")
        h_loaded = [sem(f"down_h_loaded{slot}") for slot in range(4)]
        h_hi, h_ready, k_done, added, x_loaded = (sem("down_" + q) for q in ("h_hi", "h_ready", "k_done", "added", "x_loaded"))
        squared, summed, total_ready, inverse_step, root_ready, result_ready, stored = (
            sem("down_" + q) for q in ("squared", "summed", "total_ready", "inverse_step", "root_ready",
                                       "result_ready", "stored"))
        params, mod = keep["params"], keep["mod"]
        gf0 = PARAMS["gf"][0]

        def pieces(last_block):
            if not last_block:
                return [(0, DOWN_W, LAT)]
            start = (DOWN_BLOCKS - 1) * DOWN_W
            return [(s - start, w, m) for s, w, m in segments(start, DOWN_W)]

        slots = [k % 4 if k < 16 else (k - 16) % 3 for k in range(KF)]
        slot_turns = [slots.count(slot) for slot in range(4)]
        per_block = KF - 1 + KM

        def h_slot(k):
            return slots[k], slots[:k].count(slots[k])

        def rows_since(k):
            return next(back for back in range(1, KF) if slots[(k - back) % KF] == slots[k])

        def tokens(source, block):
            return source[:, bass.ds(block * DOWN_W, DOWN_W)]

        stages = [whole[:]] + [x[:].rearrange("p m w -> p (m w)")[:, D_MODEL * q:D_MODEL * (q + 1)] for q in range(2)]

        SQUARES_AT, SUMS_AT, INVERSE_AT, ROOT_AT, RESULTS_AT, STORE_AT, RELOAD_AT = 1, 2, 11, 12, 13, 18, 21

        with nc.Block() as block_:
            @block_.sync
            def _(sp):
                def load_h(block, k):
                    slot = h_slot(k)[0]
                    sp.dma_start(h[:, slot], tokens(d["hidden_ff"][k], block)).then_inc(h_loaded[slot], 16)

                def all_tiles(source, block):
                    return source.rearrange("m p t -> p m t")[:, :, bass.ds(block * DOWN_W, DOWN_W)]

                def load_x(block):
                    sp.dma_start(x[:], all_tiles(d["x1"], block)).then_inc(x_loaded, 16)

                def store_y(block):
                    sp.wait_ge(result_ready, block * KM + KM)
                    sp.dma_start(all_tiles(d["y"], block), x[:]).then_inc(stored, 16)

                for k in range(KF):
                    if k >= 3:
                        sp.wait_ge(w_ready, k - 2)
                    sp.dma_start(stages[k % 3], d["w_down"][k]).then_inc(w_loaded[k % 3], 16)
                    if k >= 4:
                        sp.wait_ge(h_ready, k - rows_since(k) + 1)
                    load_h(0, k)
                sp.wait_ge(w_ready, KF)
                load_x(0)
                with sp.Fori(1, DOWN_BLOCKS) as block:
                    for k in range(KF):
                        sp.wait_ge(h_ready, block * KF + (k - rows_since(k) + 1))
                        load_h(block, k)
                        if k == STORE_AT:
                            store_y(block - 1)
                        if k == RELOAD_AT:
                            sp.wait_ge(stored, block * 16)
                            load_x(block)
                store_y(DOWN_BLOCKS - 1)
                sp.wait_ge(stored, DOWN_BLOCKS * 16)

            @block_.tensor
            def _(pe):
                pe.sem_inc(k_done, per_block)
                with pe.Fori(0, DOWN_BLOCKS) as block:
                    for k in range(KF):
                        pe.wait_ge(w_ready, k + 1)
                        pe.wait_ge(h_ready, block * KF + (k + 1))
                        for m in range(KM):
                            cols = slice(m * P, m * P + P)
                            if k == 0:
                                pe.wait_ge(added, block * KM + (m + 1))
                            for j, (w, v) in enumerate(((wh, hh), (wh, hl), (wl, hh))):
                                last = pe.matmul(banks[:, m, :DOWN_W], w[:, k, cols], v[:, k % 2],
                                                 start=(k == 0 and j == 0), stop=(k == KF - 1 and j == 2))
                            if k == KF - 1:
                                last.then_inc(k_done, 1)
                        if k < KF - 1:
                            last.then_inc(k_done, 1)

            @block_.scalar
            def _(act):
                def h_high(block, k):
                    slot, turn = h_slot(k)
                    act.wait_ge(h_loaded[slot], block * (16 * slot_turns[slot]) + 16 * (turn + 1))
                    act.wait_ge(k_done, block * per_block + (per_block + k - 1 if k >= 2 else (KF - 1, per_block)[k]))
                    nc.scalar.activation(hh[:, k % 2], h[:, slot], ACT.Copy).then_inc(h_hi, 1)

                def squares(block, m):
                    act.wait_ge(added, block * KM + (KM + m + 1))
                    act.wait_ge(summed, block * KM + (m + 1))
                    nc.scalar.activation(square[:], x[:, m], ACT.Square).then_inc(squared, 1)

                def root(block):
                    act.wait_ge(inverse_step, block * 2 + 2)
                    nc.scalar.activation(rstd[:], rstd[:], ACT.Sqrt).then_inc(root_ready, 1)

                for k in range(KF):
                    act.wait_ge(w_loaded[k % 3], 16 * (k // 3 + 1))
                    nc.scalar.activation(wh[:, k], stages[k % 3], ACT.Copy).then_inc(w_hi, 1)
                    h_high(0, k)
                with act.Fori(1, DOWN_BLOCKS) as block:
                    for k in range(KF):
                        h_high(block, k)
                        if SQUARES_AT <= k < SQUARES_AT + KM:
                            squares(block - 1, k - SQUARES_AT)
                        if k == ROOT_AT:
                            root(block - 1)
                for m in range(KM):
                    squares(DOWN_BLOCKS - 1, m)
                root(DOWN_BLOCKS - 1)

            @block_.gpsimd
            def _(pool):
                for block in range(DOWN_BLOCKS):
                    pool.wait_ge(summed, block * KM + (KM + 1))
                    nc.gpsimd.partition_all_reduce(rstd[:], total[:], P, bass.bass_isa.ReduceOp.add)\
                      .then_inc(total_ready, 1)

            @block_.vector
            def _(dve):
                def h_low(block, k):
                    dve.wait_ge(h_hi, block * KF + (k + 1))
                    nc.vector.tensor_tensor(hl[:, k % 2], h[:, h_slot(k)[0]], hh[:, k % 2].bitcast(F32),
                                            ALU.subtract).then_inc(h_ready, 1)

                def add_residual(block, last_block=False):
                    dve.wait_ge(x_loaded, block * 16 + 16)
                    for m in range(KM):
                        dve.wait_ge(k_done, block * per_block + (per_block + KF + m))
                        for at, w, which in pieces(last_block):
                            last = nc.vector.scalar_tensor_tensor(
                                out=x[:, m, at:at + w], in0=banks[:, m, at:at + w],
                                scalar=mod[:, GATE2 + m, which:which + 1], in1=x[:, m, at:at + w],
                                op0=ALU.mult, op1=ALU.add)
                        last.then_inc(added, 1)

                def sum_squares(block, m):
                    dve.wait_ge(squared, block * KM + (m + 1))
                    if m == 0:
                        nc.vector.tensor_copy(total[:], square[:]).then_inc(summed, 1)
                    else:
                        dve.wait_ge(summed, block * KM + (m + 1))
                        nc.vector.tensor_tensor(total[:], total[:], square[:], ALU.add).then_inc(summed, 1)

                def inverse(block):
                    dve.wait_ge(total_ready, block + 1)
                    nc.vector.tensor_scalar(rstd[:], rstd[:], 1.0 / D_MODEL, EPS, ALU.mult, ALU.add).then_inc(inverse_step, 1)
                    dve.wait_ge(inverse_step, block * 2 + 1)
                    nc.vector.reciprocal(rstd[:], rstd[:]).then_inc(inverse_step, 1)

                def result(block, m):
                    dve.wait_ge(root_ready, block + 1)
                    nc.vector.scalar_tensor_tensor(out=x[:, m], in0=x[:, m], scalar=params[:, gf0 + m:gf0 + m + 1],
                                                   in1=rstd[:], op0=ALU.mult, op1=ALU.mult).then_inc(result_ready, 1)

                dve.sem_inc(added, KM)
                dve.sem_inc(summed, 1)
                for k in range(KF):
                    dve.wait_ge(w_hi, k + 1)
                    nc.vector.tensor_tensor(wl[:, k], stages[k % 3], wh[:, k].bitcast(F32),
                                            ALU.subtract).then_inc(w_ready, 1)
                    h_low(0, k)
                with dve.Fori(1, DOWN_BLOCKS) as block:
                    for k in range(KF):
                        h_low(block, k)
                        if k == 0:
                            add_residual(block - 1)
                        if SUMS_AT <= k < SUMS_AT + KM:
                            sum_squares(block - 1, k - SUMS_AT)
                        if k == INVERSE_AT:
                            inverse(block - 1)
                        if RESULTS_AT <= k < RESULTS_AT + KM // 2:
                            for m in (2 * (k - RESULTS_AT), 2 * (k - RESULTS_AT) + 1):
                                result(block - 1, m)
                add_residual(DOWN_BLOCKS - 1, last_block=True)
                for m in range(KM):
                    sum_squares(DOWN_BLOCKS - 1, m)
                inverse(DOWN_BLOCKS - 1)
                for m in range(KM):
                    result(DOWN_BLOCKS - 1, m)



def unit_root(x, n):
    return np.exp(-2j * np.pi * (x % n) / n)


def latent_tables():
    b = np.arange(64)
    first = np.zeros((2, 32, 4, 32, 2, 4))
    for half in range(2):
        a = np.arange(32) + 32 * half
        for k in range(32):
            re = unit_root(a * k, 64).real
            im = unit_root(a * k, 64).imag if k else unit_root(a * 32, 64).real
            for q in range(4):
                first[half, :, q, k, 0, q], first[half, :, q, k, 1, q] = re, im
    second = np.zeros((32, 2, 64, 2, 64))
    back1 = np.zeros((32, 2, 64, 2, 64))
    for k in range(1, 32):
        w = unit_root(b * k, 4096)[:, None] * unit_root(np.outer(b, b), 64)
        second[k, 0, :, 0], second[k, 1, :, 0], second[k, 0, :, 1], second[k, 1, :, 1] = w.real, -w.imag, w.imag, w.real
        w = w.T
        back1[k, 0, :, 0], back1[k, 1, :, 0], back1[k, 1, :, 1], back1[k, 0, :, 1] = w.real, w.imag, w.real, -w.imag
    w = unit_root(32 * b, 4096)[:, None] * unit_root(np.outer(b, np.arange(32)), 64)
    second[0, 1, :, 0, :32], second[0, 1, :, 1, :32] = w.real, w.imag
    back1[0, 0, :32, 1], back1[0, 1, :32, 1] = 2 * w.real.T, 2 * w.imag.T
    second[0, 0, :, 0, 32], second[0, 0, :, 1, 32] = 1, (-1.0) ** b
    back1[0, 0, 32, 0], back1[0, 1, 32, 0] = 1, (-1.0) ** b
    w = unit_root(np.outer(b, np.arange(1, 32)), 64)
    second[0, 0, :, 0, 33:], second[0, 0, :, 1, 33:] = w.real, w.imag
    back1[0, 0, 33:, 0], back1[0, 1, 33:, 0] = 2 * w.real.T, 2 * w.imag.T
    r = np.arange(64)
    second = second[:, :, r // 4 + 16 * (r % 4)]
    back2 = np.zeros((32, 2, 2, 32, 2))
    a = np.arange(32)
    for k in range(32):
        re = 2 * np.cos(2 * np.pi * a * k / 64) if k else np.ones(32)
        im = -2 * np.sin(2 * np.pi * a * k / 64) if k else (-1.0) ** a
        for half in range(2):
            back2[k, 0, half, :, half], back2[k, 1, half, :, half] = re / 4096, im / 4096
    return (first.reshape(2, P, 256).transpose(1, 0, 2), second.reshape(32, P, P).transpose(1, 0, 2),
            back1.reshape(32, P, P).transpose(1, 0, 2), back2.reshape(P, 64))


def context_tables():
    n, k = np.arange(256), np.arange(128)
    w = unit_root(np.outer(n, k), 256)
    re, im = w.real.copy(), w.imag.copy()
    im[:, 0] = (-1.0) ** n
    forward = np.stack([re, im], 1).reshape(2, P, 2, P)
    back_re, back_im = 2 * w.real.T[:, :P] / 256, 2 * w.imag.T[:, :P] / 256
    back_re[0] /= 2
    back_im[0] = (-1.0) ** n[:P] / 256
    return forward.transpose(1, 0, 2, 3), np.stack([back_re, back_im], 1)


def filter_tables():
    f32 = np.float32
    deltas = np.abs(np.linspace(math.log(1e-2) / 1.5, math.log(1e-2) / 0.3, D_HY, dtype=f32))
    bands = np.linspace(1e-4, HY_BANDS - 1, HY_BANDS, dtype=f32)
    feats, decay = np.zeros((P, POS), f32), np.zeros((CT, P, ROW_TILES, P), f32)
    m = np.arange(P)
    for rt in range(ROW_TILES):
        if rt < 32:
            length, n = SEQ_LAT, 2048 * (rt % 2) + 16 * m + rt // 2
        else:
            length, n = SEQ_CTX, 128 * (rt - 32) + m
        pos = np.where(n < length, n, 2 * length - n).astype(f32)
        t = pos / f32(length - 1)
        omega = f32(2.0 * math.pi) * pos / f32(length)
        angle = omega[:, None] * bands[None, :]
        feats[:1 + 2 * HY_BANDS, rt * P:rt * P + P] = np.concatenate([t[:, None], np.cos(angle), np.sin(angle)], 1).T
        row = np.exp(-t[:, None] * deltas[None, :])
        row[n == length] = 0.0
        decay[:, :, rt, :] = row.reshape(P, CT, P).transpose(1, 0, 2)
    return feats, decay



def build(nc, d):
    with ExitStack() as ctx:
        def sem(name):
            return ctx.enter_context(nc.semaphore(name))

        keep = {name: ctx.enter_context(nc.sbuf_tensor(name, shape, F32)) for name, shape in (
            ("params", [P, N_PARAMS]), ("mod", [P, N_MOD * KM, 2]), ("scale1", [P, KM, 2]), ("scale2", [P, KM, 2]),
            ("sp8", [P, 2 * CT]), ("nsp8", [P, 2 * CT]), ("ident", [P, P]), ("ones", [P, P]),
            ("zero", [P, 1]))}
        keep["norm_sems"] = norm_semaphores(sem)
        modulation(nc, sem, d, keep)
        in_proj(nc, sem, d, keep)
        rglru(nc, sem, d, keep)
        hyena(nc, sem, d, keep)
        out_proj(nc, sem, d, keep)
        ffn_up(nc, sem, d, keep)
        ffn_down(nc, sem, d, keep)


def columns(a):
    a = np.asarray(a)
    return np.ascontiguousarray(a.reshape(-1, P).T)


def pad_column(a):
    return np.concatenate([np.asarray(a), np.zeros_like(a)], -1)


def units(w, order=None):
    k, n = w.shape
    u = w.reshape(k // P, P, n // P, P).transpose(2, 1, 0, 3)
    return np.ascontiguousarray(u if order is None else u[order])


def layout(x_prompt, x_sample, state_rglru, c, c_ctx, w_ada, b_ada, g_norm1, g_norm2, w_in, rg_conv_w, rg_conv_b,
           rg_gate_w, rg_gate_b, rg_a, hy_conv_w, hy_conv_b, hf_w1, hf_b1, hf_w2, hf_b2, hf_w3, hf_freq, hy_bias,
           g_rnn_out, g_hy_out, w_out, w_up, ffn_conv_w, ffn_conv_b, w_down, g_final):
    f32 = np.float32
    order_in = list(range(CT)) + list(range(2 * CT, 5 * CT)) + list(range(CT, 2 * CT))
    conv_w = np.concatenate([rg_conv_w[0], np.concatenate([np.zeros((1, 3 * D_HY), f32), hy_conv_w[0]], 0)], 1)
    parts = {
        "g1": columns(g_norm1[0]), "g2": columns(g_norm2[0]), "gf": columns(g_final),
        "go": np.concatenate([columns(g_rnn_out[0]), columns(g_hy_out[0])], 1),
        "cw": np.ascontiguousarray(conv_w.reshape(4, N_CONV, P).transpose(2, 1, 0)).reshape(P, 4 * N_CONV),
        "cb": np.concatenate([columns(rg_conv_b[0]), columns(hy_conv_b[0])], 1),
        "gate_b": columns(rg_gate_b[0]), "rg_a": columns(rg_a[0]), "h0": columns(state_rglru[0, 0]),
        "hy_b": columns(hy_bias[0]), "ffn_w": columns(ffn_conv_w[0]), "ffn_b": columns(ffn_conv_b[0]),
        "mlp_b": columns(np.concatenate([pad_column(hf_b1[0]), pad_column(hf_b2[0])])),
        "mlp_f": columns(pad_column(hf_freq[0])),
    }
    first, second, back1, back2 = latent_tables()
    ctx_forward, ctx_back = context_tables()
    feats, decay = filter_tables()
    up = units(w_up[0])
    arrays = {
        "xT": np.concatenate([x_sample[0], x_prompt[0]], 0).T.reshape(KM, P, T),
        "cond": np.stack([c[0].reshape(KM, P), c_ctx.reshape(KM, P)], -1).transpose(1, 0, 2),
        "params": np.concatenate([parts[name] for name in PARAMS], 1),
        "ada_bias": np.stack([b_ada[0], b_ada[0]]),
        "w_ada": w_ada[0].reshape(KM, P, 12, 512).transpose(2, 1, 0, 3),
        "w_in": units(w_in[0], order_in),
        "gate_w": rg_gate_w[0].reshape(4, CT, 2, 64, 64).transpose(2, 3, 0, 1, 4).reshape(2, 64, 4 * CT, 64),
        "mlp_w1": hf_w1[0], "mlp_w2": hf_w2[0],
        "mlp_w3": hf_w3[0].reshape(64, 2, 2, CT, P).transpose(1, 3, 0, 2, 4),
        "w_out": units(w_out[0]),
        "w_up": np.concatenate([up[:1], up[KF:KF + 1], np.stack([up[KF + 1:], up[1:KF]], 1).reshape(-1, P, KM, P)]),
        "w_down": w_down[0].reshape(KF, P, D_MODEL),
        "ident": np.eye(P, dtype=f32), "feats": feats, "decay": decay,
        "first_table": first.astype(f32), "second_table": second.astype(f32), "back1_table": back1.astype(f32),
        "back2_table": back2.astype(f32), "ctx_forward_table": ctx_forward.astype(f32),
        "ctx_back_table": ctx_back.astype(f32),
    }
    return {name: np.ascontiguousarray(a) for name, a in arrays.items()}


SCRATCH = {"pre": [N_IN, P, T], "mixed": [KM, P, T], "x1": [KM, P, T], "hidden_ff": [KF, P, T], "hidden": [P, POS]}
OUTPUTS = {"y": [KM, P, T], "states": [P, CT, 2]}


def kernel(**inputs):
    import concourse.bacc as bacc
    from concourse.bass_utils import run_bass_kernel_spmd

    nc = bacc.Bacc("TRN2", target_bir_lowering=False, num_devices=1)
    arrays = layout(**{name: np.asarray(a) for name, a in inputs.items()})
    d = {name: nc.dram_tensor(name + "_in", list(a.shape), F32, kind="ExternalInput").ap() for name, a in arrays.items()}
    d.update({name: nc.dram_tensor(name + "_dram", shape, F32, kind="Internal").ap() for name, shape in SCRATCH.items()})
    d.update({name: nc.dram_tensor(name + "_out", shape, F32, kind="ExternalOutput").ap()
              for name, shape in OUTPUTS.items()})
    build(nc, d)
    r = run_bass_kernel_spmd(nc, [{name + "_in": a for name, a in arrays.items()}], core_ids=[0])
    y = r.results[0]["y_out"].reshape(D_MODEL, T).T
    states = r.results[0]["states_out"].transpose(2, 1, 0).reshape(1, 1, 2, D_RNN)
    return (np.ascontiguousarray(y[SEQ_LAT:])[None], np.ascontiguousarray(y[:SEQ_LAT])[None],
            np.ascontiguousarray(states))
```
